# Optimizing a Trainium2 kernel written in Bass

```python
import jax, jax.numpy as jnp
from jax import lax
import numpy as np

D_MODEL = 1024
BATCH = 1
SEQ = 512
DEPTH = 2

CTX_LEN = 256
GRID_W = 64
HEAD_DIM = 64
NA_HEADS = 6
NA_KR = 8
NA_KW = 16
NA_QB = 16
NA_SPAN = NA_QB + NA_KW
SWA_HEADS = 6
SWA_KV_HEADS = 2
SWA_WINDOW = 128
SWA_BLOCK = 128
FNET_GROUPS = 4
FNET_GROUP_DIM = 64
NA_WIDTH = NA_HEADS * HEAD_DIM
SWA_WIDTH = SWA_HEADS * HEAD_DIM
SWA_KV_WIDTH = SWA_KV_HEADS * HEAD_DIM
FNET_WIDTH = FNET_GROUPS * FNET_GROUP_DIM
D_MIX = NA_WIDTH + SWA_WIDTH + FNET_WIDTH
D_IN = 3 * NA_WIDTH + SWA_WIDTH + 2 * SWA_KV_WIDTH + FNET_WIDTH
IN_SPLITS = (NA_WIDTH, 2 * NA_WIDTH, 3 * NA_WIDTH, 3 * NA_WIDTH + SWA_WIDTH,
             3 * NA_WIDTH + SWA_WIDTH + SWA_KV_WIDTH, 3 * NA_WIDTH + SWA_WIDTH + 2 * SWA_KV_WIDTH)
D_FF = 256 * ((8 * D_MODEL // 3 + 255) // 256)
N_SUB = 3
N_MOD = 3 * N_SUB
MACARON_WEIGHT = 0.5
ROPE_BASE = 10000.0
RMS_EPS = 1e-6
NEG_INF = -1e30


def rms_norm(x, g):
    x32 = x.astype(jnp.float32)
    y = x32 * lax.rsqrt(jnp.mean(x32 * x32, axis=-1, keepdims=True) + RMS_EPS)
    return (y * g.astype(jnp.float32)).astype(x.dtype)

def modulate(h, shift, scale):
    return h * (1 + scale) + shift

def swiglu(h, w1, w2):
    gate, up = jnp.split(h @ w1, 2, axis=-1)
    return (jax.nn.silu(gate) * up) @ w2

def rope_half(x, pos):
    half = x.shape[-1] // 2
    inv = ROPE_BASE ** (-jnp.arange(half, dtype=jnp.float32) / half)
    ang = pos[:, None] * inv[None, :]
    cos = jnp.cos(ang)[:, None, :]
    sin = jnp.sin(ang)[:, None, :]
    x1, x2 = x[..., :half], x[..., half:]
    return jnp.concatenate([x1 * cos - x2 * sin, x1 * sin + x2 * cos], axis=-1)

def axial_rope(x):
    s = x.shape[1]
    t = jnp.arange(s)
    rows = (t // GRID_W).astype(jnp.float32)
    cols = (t % GRID_W).astype(jnp.float32)
    x32 = x.astype(jnp.float32)
    a = x.shape[-1] // 2
    out = jnp.concatenate([rope_half(x32[..., :a], rows), rope_half(x32[..., a:], cols)], axis=-1)
    return out.astype(x.dtype)

def _na_column_tables():
    n_jb = GRID_W // NA_QB
    k_start = np.clip(np.arange(n_jb) * NA_QB - NA_KW // 2, 0, GRID_W - NA_SPAN)
    col_idx = k_start[:, None] + np.arange(NA_SPAN)[None, :]
    q_col = np.arange(n_jb)[:, None] * NA_QB + np.arange(NA_QB)[None, :]
    w_start = np.clip(q_col - NA_KW // 2, 0, GRID_W - NA_KW)[..., None]
    k_col = col_idx[:, None, :]
    valid = (k_col >= w_start) & (k_col < w_start + NA_KW)
    offset = np.clip(k_col - q_col[..., None] + NA_KW - 1, 0, 2 * NA_KW - 2)
    return col_idx, valid, offset

def neighbourhood_attention(q, k, v, kc, vc, rpb):
    b, s, h, hd = q.shape
    rows = s // GRID_W
    kr = min(NA_KR, rows)
    n_jb = GRID_W // NA_QB
    n_lat = kr * NA_SPAN
    scale = hd ** -0.5
    col_idx, col_valid, col_off = _na_column_tables()
    qg = q.reshape(b, rows, n_jb, NA_QB, h, hd)
    kg = k.reshape(b, rows, GRID_W, h, hd)[:, :, col_idx]
    vg = v.reshape(b, rows, GRID_W, h, hd)[:, :, col_idx]
    rpb_col = rpb[:, :, col_off]
    valid = jnp.asarray(col_valid)[None, None, :, :, None, :]

    def row_step(r):
        rs = jnp.clip(r - kr // 2, 0, rows - kr)
        q_r = lax.dynamic_index_in_dim(qg, r, axis=1, keepdims=False)
        k_r = lax.dynamic_slice_in_dim(kg, rs, kr, axis=1)
        v_r = lax.dynamic_slice_in_dim(vg, rs, kr, axis=1)
        row_off = rs + jnp.arange(kr) - r + NA_KR - 1
        bias = jnp.transpose(rpb_col[:, row_off], (0, 2, 3, 1, 4)).astype(jnp.float32)
        s_lat = jnp.einsum('bjqhd,bijshd->bhjqis', q_r, k_r).astype(jnp.float32) * scale + bias
        s_lat = jnp.where(valid, s_lat, NEG_INF).reshape(b, h, n_jb, NA_QB, n_lat)
        s_ctx = jnp.einsum('bjqhd,blhd->bhjql', q_r, kc).astype(jnp.float32) * scale
        p = jax.nn.softmax(jnp.concatenate([s_lat, s_ctx], axis=-1), axis=-1).astype(v.dtype)
        p_lat = p[..., :n_lat].reshape(b, h, n_jb, NA_QB, kr, NA_SPAN)
        p_ctx = p[..., n_lat:]
        return (jnp.einsum('bhjqis,bijshd->bjqhd', p_lat, v_r)
                + jnp.einsum('bhjql,blhd->bjqhd', p_ctx, vc))

    out = lax.map(row_step, jnp.arange(rows))
    return jnp.moveaxis(out, 0, 1).reshape(b, s, h * hd)

def window_gqa_attention(q, k, v, kc, vc, sink):
    b, s, h, hd = q.shape
    kvh = k.shape[2]
    g = h // kvh
    n_ctx = kc.shape[1]
    nb = s // SWA_BLOCK
    span = 3 * SWA_BLOCK
    scale = hd ** -0.5
    qb = q.reshape(b, nb, SWA_BLOCK, kvh, g, hd)
    pad = ((0, 0), (SWA_BLOCK, SWA_BLOCK), (0, 0), (0, 0))
    kp = jnp.pad(k, pad)
    vp = jnp.pad(v, pad)
    rel = jnp.arange(span)[None, :] - SWA_BLOCK - jnp.arange(SWA_BLOCK)[:, None]
    in_window = jnp.abs(rel) <= SWA_WINDOW
    sink_l = jnp.broadcast_to(sink.astype(jnp.float32).reshape(1, kvh, g, 1, 1), (b, kvh, g, SWA_BLOCK, 1))

    def block_step(n):
        q_n = lax.dynamic_index_in_dim(qb, n, axis=1, keepdims=False)
        k_n = lax.dynamic_slice_in_dim(kp, n * SWA_BLOCK, span, axis=1)
        v_n = lax.dynamic_slice_in_dim(vp, n * SWA_BLOCK, span, axis=1)
        kpos = (n - 1) * SWA_BLOCK + jnp.arange(span)
        valid = in_window & ((kpos >= 0) & (kpos < s))[None, :]
        s_lat = jnp.einsum('bqkgd,bskd->bkgqs', q_n, k_n).astype(jnp.float32) * scale
        s_lat = jnp.where(valid, s_lat, NEG_INF)
        s_ctx = jnp.einsum('bqkgd,blkd->bkgql', q_n, kc).astype(jnp.float32) * scale
        p = jax.nn.softmax(jnp.concatenate([s_lat, s_ctx, sink_l], axis=-1), axis=-1).astype(v.dtype)
        return (jnp.einsum('bkgqs,bskd->bqkgd', p[..., :span], v_n)
                + jnp.einsum('bkgql,blkd->bqkgd', p[..., span:span + n_ctx], vc))

    out = lax.map(block_step, jnp.arange(nb))
    return jnp.moveaxis(out, 0, 1).reshape(b, s, h * hd)

def context_attention(qc, kc, vc, sink=None):
    b, l, h, hd = qc.shape
    kvh = kc.shape[2]
    g = h // kvh
    q5 = qc.reshape(b, l, kvh, g, hd)
    sc = jnp.einsum('blkgd,bmkd->bkglm', q5, kc).astype(jnp.float32) * hd ** -0.5
    if sink is not None:
        sk = jnp.broadcast_to(sink.astype(jnp.float32).reshape(1, kvh, g, 1, 1), (b, kvh, g, l, 1))
        sc = jnp.concatenate([sc, sk], axis=-1)
    p = jax.nn.softmax(sc, axis=-1)[..., :l].astype(vc.dtype)
    return jnp.einsum('bkglm,bmkd->blkgd', p, vc).reshape(b, l, h * hd)

def fourier_mix(u):
    b, n, _ = u.shape
    u4 = u.astype(jnp.float32).reshape(b, n, FNET_GROUPS, FNET_GROUP_DIM)
    f = jnp.fft.fft2(u4, axes=(1, 3), norm='ortho').real
    return f.reshape(b, n, FNET_WIDTH).astype(u.dtype)

def project_groups(h, w_in):
    b, n, _ = h.shape
    aq, ak, av, bq, bk, bv, fu = jnp.split(h @ w_in, IN_SPLITS, axis=-1)
    heads = lambda t, nh: t.reshape(b, n, nh, HEAD_DIM)
    return (heads(aq, NA_HEADS), heads(ak, NA_HEADS), heads(av, NA_HEADS),
            heads(bq, SWA_HEADS), heads(bk, SWA_KV_HEADS), heads(bv, SWA_KV_HEADS), fu)

def mods_of(m, sub):
    return m[..., 3 * sub, :], m[..., 3 * sub + 1, :], m[..., 3 * sub + 2, :]

def ffn_sublayer(h, m, sub, g_pre, g_post, w1, w2):
    shift, scale, gate = mods_of(m, sub)
    y = swiglu(modulate(rms_norm(h, g_pre[sub]), shift, scale), w1, w2)
    return h + MACARON_WEIGHT * gate * rms_norm(y, g_post[sub])

def hybrid_layer(x, xc, mod, mod_c, g_pre, g_post, w_ffn_in, w_ffn_out, w_in, w_out, na_rpb, swa_sink, ctx_out):
    x = ffn_sublayer(x, mod, 0, g_pre, g_post, w_ffn_in[0], w_ffn_out[0])
    xc = ffn_sublayer(xc, mod_c, 0, g_pre, g_post, w_ffn_in[0], w_ffn_out[0])
    sh, sc, gt = mods_of(mod, 1)
    shc, scc, gtc = mods_of(mod_c, 1)
    h = modulate(rms_norm(x, g_pre[1]), sh, sc)
    hc = modulate(rms_norm(xc, g_pre[1]), shc, scc)
    aq, ak, av, bq, bk, bv, fu = project_groups(h, w_in)
    aqc, akc, avc, bqc, bkc, bvc, fuc = project_groups(hc, w_in)
    bq = axial_rope(bq)
    bk = axial_rope(bk)
    o_a = neighbourhood_attention(aq, ak, av, akc, avc, na_rpb)
    o_b = window_gqa_attention(bq, bk, bv, bkc, bvc, swa_sink)
    o_c = fourier_mix(fu)
    o = jnp.concatenate([o_a, o_b, o_c], axis=-1) @ w_out
    x = x + gt * rms_norm(o, g_post[1])
    x = ffn_sublayer(x, mod, 2, g_pre, g_post, w_ffn_in[1], w_ffn_out[1])
    if ctx_out:
        oc = jnp.concatenate([context_attention(aqc, akc, avc),
                              context_attention(bqc, bkc, bvc, swa_sink),
                              fourier_mix(fuc)], axis=-1) @ w_out
        xc = xc + gtc * rms_norm(oc, g_post[1])
        xc = ffn_sublayer(xc, mod_c, 2, g_pre, g_post, w_ffn_in[1], w_ffn_out[1])
    else:
        xc = None
    return x, xc

def first_inputs(seed: int = 0) -> dict:
    key = jax.random.key(seed)
    ks = jax.random.split(key, 14)
    nrm = jax.random.normal
    f32 = jnp.float32
    return {
        'x': nrm(ks[0], (BATCH, SEQ, D_MODEL), f32),
        'c': nrm(ks[1], (BATCH, D_MODEL), f32),
        'ctx': nrm(ks[2], (BATCH, CTX_LEN, D_MODEL), f32),
        'c_ctx': nrm(ks[3], (D_MODEL,), f32),
        'w_mod': nrm(ks[4], (DEPTH, D_MODEL, N_MOD * D_MODEL), f32) * (0.5 * D_MODEL ** -0.5),
        'b_mod': nrm(ks[5], (DEPTH, N_MOD * D_MODEL), f32) * 0.01,
        'g_pre': 1.0 + 0.01 * nrm(ks[6], (DEPTH, N_SUB, D_MODEL), f32),
        'g_post': 1.0 + 0.01 * nrm(ks[7], (DEPTH, N_SUB, D_MODEL), f32),
        'w_ffn_in': nrm(ks[8], (DEPTH, 2, D_MODEL, 2 * D_FF), f32) * D_MODEL ** -0.5,
        'w_ffn_out': nrm(ks[9], (DEPTH, 2, D_FF, D_MODEL), f32) * D_FF ** -0.5,
        'w_in': nrm(ks[10], (DEPTH, D_MODEL, D_IN), f32) * D_MODEL ** -0.5,
        'w_out': nrm(ks[11], (DEPTH, D_MIX, D_MODEL), f32) * D_MIX ** -0.5,
        'na_rpb': nrm(ks[12], (DEPTH, NA_HEADS, 2 * NA_KR - 1, 2 * NA_KW - 1), f32) * 0.1,
        'swa_sink': nrm(ks[13], (DEPTH, SWA_HEADS), f32) * 0.5,
    }

def first_block(x, c, ctx, c_ctx, w_mod, b_mod, g_pre, g_post, w_ffn_in, w_ffn_out, w_in, w_out, na_rpb, swa_sink):
    b = x.shape[0]
    xc = ctx
    c_act = jax.nn.silu(c)
    cc_act = jax.nn.silu(c_ctx)
    for layer in range(DEPTH):
        mod = (c_act @ w_mod[layer] + b_mod[layer]).reshape(b, 1, N_MOD, D_MODEL)
        mod_c = (cc_act @ w_mod[layer] + b_mod[layer]).reshape(N_MOD, D_MODEL)
        x, xc = hybrid_layer(x, xc, mod, mod_c, g_pre[layer], g_post[layer], w_ffn_in[layer], w_ffn_out[layer],
                             w_in[layer], w_out[layer], na_rpb[layer], swa_sink[layer],
                             ctx_out=(layer < DEPTH - 1))
    return x


CHUNK = 64
N_META = 16
EPS = 1e-6
N_EVEN = (DEPTH + 1) // 2
N_ODD = DEPTH // 2
CONV_W = 4

LRU_WIDTH = D_MODEL
LRU_BLOCKS = 4
LRU_BLOCK = LRU_WIDTH // LRU_BLOCKS
RG_LRU_C = 8.0

SSD_WIDTH = D_MODEL
SSD_HEAD_DIM = 64
SSD_HEADS = SSD_WIDTH // SSD_HEAD_DIM
SSD_GROUPS = 2
SSD_HPG = SSD_HEADS // SSD_GROUPS
SSD_STATE = 128
SSD_CHUNK = CHUNK
SSD_CONV_DIM = SSD_WIDTH + 2 * SSD_GROUPS * SSD_STATE

EVEN_SPLITS = (LRU_WIDTH, 2 * LRU_WIDTH, 2 * LRU_WIDTH + SSD_WIDTH,
               2 * LRU_WIDTH + SSD_WIDTH + SSD_CONV_DIM)
EVEN_IN = 2 * LRU_WIDTH + SSD_WIDTH + SSD_CONV_DIM + SSD_HEADS
EVEN_MIX = LRU_WIDTH + SSD_WIDTH

SB_HEADS = 16
SB_HEAD_DIM = D_MODEL // SB_HEADS
SB_WIDTH = SB_HEADS * SB_HEAD_DIM
SB_BLOCK = 128
ODD_IN = 4 * SB_WIDTH


def rmsnorm(x, w):
    xf = x.astype(jnp.float32)
    y = xf * lax.rsqrt(jnp.mean(xf * xf, axis=-1, keepdims=True) + EPS)
    return (y * w.astype(jnp.float32)).astype(x.dtype)

def causal_dwconv(u, w, b):
    out = lax.conv_general_dilated(
        u, w[:, None, :].astype(u.dtype), window_strides=(1,),
        padding=[(CONV_W - 1, 0)], dimension_numbers=('NWC', 'WIO', 'NWC'),
        feature_group_count=u.shape[-1])
    return out + b

def linear_scan(a, b):
    def combine(left, right):
        al, bl = left
        ar, br = right
        return al * ar, ar * bl + br
    _, h = lax.associative_scan(combine, (a, b), axis=1)
    return h

def rg_lru(u, w_a, b_a, w_x, b_x, lam):
    bsz, L, _ = u.shape
    uf = u.astype(jnp.float32)
    ub = uf.reshape(bsz, L, LRU_BLOCKS, LRU_BLOCK)
    r = jax.nn.sigmoid(jnp.einsum('blgi,gij->blgj', ub, w_a).reshape(bsz, L, LRU_WIDTH) + b_a)
    i = jax.nn.sigmoid(jnp.einsum('blgi,gij->blgj', ub, w_x).reshape(bsz, L, LRU_WIDTH) + b_x)
    log_a = -RG_LRU_C * r * jax.nn.softplus(-lam)
    a = jnp.exp(log_a)
    mult = jnp.sqrt(-jnp.expm1(2.0 * log_a))
    return linear_scan(a, mult * i * uf)

def ssd_scan(xh, dt, a, bmat, cmat):
    bsz, L, _, _ = xh.shape
    pad = (-L) % SSD_CHUNK
    def padf(t):
        return jnp.pad(t, [(0, 0), (pad, 0)] + [(0, 0)] * (t.ndim - 2))
    f32 = jnp.float32
    xdt = padf((xh * dt[..., None]).astype(f32))
    adt = padf((dt * a).astype(f32))
    bm = padf(bmat.astype(f32))
    cm = padf(cmat.astype(f32))
    nc = (L + pad) // SSD_CHUNK
    X = xdt.reshape(bsz, nc, SSD_CHUNK, SSD_GROUPS, SSD_HPG, SSD_HEAD_DIM)
    A = adt.reshape(bsz, nc, SSD_CHUNK, SSD_GROUPS, SSD_HPG).transpose(0, 3, 4, 1, 2)
    Bc = bm.reshape(bsz, nc, SSD_CHUNK, SSD_GROUPS, SSD_STATE)
    Cc = cm.reshape(bsz, nc, SSD_CHUNK, SSD_GROUPS, SSD_STATE)
    a_cum = jnp.cumsum(A, axis=-1)
    tri = jnp.tril(jnp.ones((SSD_CHUNK, SSD_CHUNK), bool))
    seg = a_cum[..., :, None] - a_cum[..., None, :]
    decay = jnp.exp(jnp.where(tri, seg, -jnp.inf))
    cb = jnp.einsum('bclgn,bcsgn->bcgls', Cc, Bc)
    y_diag = jnp.einsum('bcgls,bgecls,bcsgep->bclgep', cb, decay, X)
    decay_states = jnp.exp(a_cum[..., -1:] - a_cum)
    states = jnp.einsum('bclgn,bgecl,bclgep->bcgepn', Bc, decay_states, X)
    chunk_tot = jnp.pad(a_cum[..., -1], [(0, 0), (0, 0), (0, 0), (1, 0)])
    cs = jnp.cumsum(chunk_tot, axis=-1)
    tri_c = jnp.tril(jnp.ones((nc + 1, nc + 1), bool))
    decay_chunk = jnp.exp(jnp.where(tri_c, cs[..., :, None] - cs[..., None, :], -jnp.inf))
    states = jnp.concatenate([jnp.zeros_like(states[:, :1]), states], axis=1)
    states = jnp.einsum('bgezc,bcgepn->bzgepn', decay_chunk, states)[:, :-1]
    y_off = jnp.einsum('bclgn,bcgepn,bgecl->bclgep', Cc, states, jnp.exp(a_cum))
    y = (y_diag + y_off).reshape(bsz, L + pad, SSD_HEADS, SSD_HEAD_DIM)
    return y[:, pad:]

def gated_group_rmsnorm(y, z, w):
    bsz, L, W = y.shape
    g = (y * jax.nn.silu(z.astype(jnp.float32))).reshape(bsz, L, SSD_GROUPS, W // SSD_GROUPS)
    g = g * lax.rsqrt(jnp.mean(g * g, axis=-1, keepdims=True) + EPS)
    return g.reshape(bsz, L, W) * w.astype(jnp.float32)

def rglru_ssd_layer(h, norm_w, w_in, lru_conv_w, lru_conv_b, lru_w_a, lru_b_a,
                    lru_w_x, lru_b_x, lru_lambda, ssd_conv_w, ssd_conv_b,
                    ssd_dt_bias, ssd_a_log, ssd_d, ssd_norm, w_out):
    bsz, L, _ = h.shape
    u = rmsnorm(h, norm_w)
    proj = u @ w_in
    lru_x, lru_g, ssd_z, ssd_xbc, ssd_dt = jnp.split(proj, EVEN_SPLITS, axis=-1)
    lx = causal_dwconv(lru_x, lru_conv_w, lru_conv_b)
    y_a = rg_lru(lx, lru_w_a, lru_b_a, lru_w_x, lru_b_x, lru_lambda) * jax.nn.silu(lru_g.astype(jnp.float32))
    xbc = jax.nn.silu(causal_dwconv(ssd_xbc, ssd_conv_w, ssd_conv_b))
    xs, bm, cm = jnp.split(xbc, (SSD_WIDTH, SSD_WIDTH + SSD_GROUPS * SSD_STATE), axis=-1)
    dt = jax.nn.softplus(ssd_dt.astype(jnp.float32) + ssd_dt_bias)
    a = -jnp.exp(ssd_a_log.astype(jnp.float32))
    xh = xs.reshape(bsz, L, SSD_HEADS, SSD_HEAD_DIM)
    y = ssd_scan(xh, dt, a,
                 bm.reshape(bsz, L, SSD_GROUPS, SSD_STATE),
                 cm.reshape(bsz, L, SSD_GROUPS, SSD_STATE))
    y = y + xh.astype(jnp.float32) * ssd_d[:, None]
    y_b = gated_group_rmsnorm(y.reshape(bsz, L, SSD_WIDTH), ssd_z, ssd_norm)
    mixed = jnp.concatenate([y_a, y_b], axis=-1).astype(h.dtype)
    return h + mixed @ w_out

def stick_breaking_block(q_blk, k_ctx, v_ctx, q0):
    tq = q_blk.shape[1]
    s_len = k_ctx.shape[1]
    z = jnp.einsum('bthd,bshd->bhts', q_blk.astype(jnp.float32),
                   k_ctx.astype(jnp.float32)) * (SB_HEAD_DIM ** -0.5)
    before = jnp.arange(s_len)[None, :] < (q0 + jnp.arange(tq))[:, None]
    log_keep = jnp.where(before, jax.nn.log_sigmoid(-z), 0.0)
    csum = jnp.cumsum(log_keep, axis=-1)
    weights = jnp.where(before, jnp.exp(jax.nn.log_sigmoid(z) + csum[..., -1:] - csum), 0.0)
    return jnp.einsum('bhts,bshd->bthd', weights, v_ctx.astype(jnp.float32))

def stick_breaking_layer(h, norm_w, w_in, w_out):
    bsz, L, _ = h.shape
    u = rmsnorm(h, norm_w)
    q, k, v, g = jnp.split(u @ w_in, 4, axis=-1)
    q = q.reshape(bsz, L, SB_HEADS, SB_HEAD_DIM)
    k = k.reshape(bsz, L, SB_HEADS, SB_HEAD_DIM)
    v = v.reshape(bsz, L, SB_HEADS, SB_HEAD_DIM)
    bounds = [0] + list(range(N_META, L, SB_BLOCK)) + [L]
    outs = [stick_breaking_block(q[:, s:e], k[:, :e], v[:, :e], s)
            for s, e in zip(bounds[:-1], bounds[1:])]
    o = jnp.concatenate(outs, axis=1).reshape(bsz, L, SB_WIDTH)
    o = (o * jax.nn.silu(g.astype(jnp.float32))).astype(h.dtype)
    return h + o @ w_out

def second_inputs(seed: int = 0) -> dict:
    key = jax.random.key(seed)
    ks = jax.random.split(key, 24)
    f32 = jnp.float32

    def nrm(k, shape, fan_in):
        return jax.random.normal(k, shape, f32) * (fan_in ** -0.5)

    def gain(k, shape):
        return 1.0 + 0.05 * jax.random.normal(k, shape, f32)

    def bias(k, shape, s=0.05):
        return s * jax.random.normal(k, shape, f32)

    x = jax.random.normal(ks[0], (BATCH, SEQ, D_MODEL), f32)
    meta = jax.random.normal(ks[1], (N_META, D_MODEL), f32)
    even_norm = gain(ks[2], (N_EVEN, D_MODEL))
    even_w_in = nrm(ks[3], (N_EVEN, D_MODEL, EVEN_IN), D_MODEL)
    lru_conv_w = nrm(ks[4], (N_EVEN, CONV_W, LRU_WIDTH), CONV_W)
    lru_conv_b = bias(ks[5], (N_EVEN, LRU_WIDTH))
    lru_w_a = nrm(ks[6], (N_EVEN, LRU_BLOCKS, LRU_BLOCK, LRU_BLOCK), LRU_BLOCK)
    lru_b_a = bias(ks[7], (N_EVEN, LRU_WIDTH), 0.1)
    lru_w_x = nrm(ks[8], (N_EVEN, LRU_BLOCKS, LRU_BLOCK, LRU_BLOCK), LRU_BLOCK)
    lru_b_x = bias(ks[9], (N_EVEN, LRU_WIDTH), 0.1)
    a_c = jax.random.uniform(ks[10], (N_EVEN, LRU_WIDTH), f32, minval=0.9, maxval=0.999)
    a0 = a_c ** (1.0 / RG_LRU_C)
    lru_lambda = jnp.log(a0) - jnp.log1p(-a0)
    ssd_conv_w = nrm(ks[11], (N_EVEN, CONV_W, SSD_CONV_DIM), CONV_W)
    ssd_conv_b = bias(ks[12], (N_EVEN, SSD_CONV_DIM))
    dt0 = jnp.exp(jax.random.uniform(ks[13], (N_EVEN, SSD_HEADS), f32,
                                     minval=float(np.log(1e-3)), maxval=float(np.log(1e-1))))
    ssd_dt_bias = dt0 + jnp.log(-jnp.expm1(-dt0))
    ssd_a_log = jnp.log(jax.random.uniform(ks[14], (N_EVEN, SSD_HEADS), f32, minval=1.0, maxval=16.0))
    ssd_d = gain(ks[15], (N_EVEN, SSD_HEADS))
    ssd_norm = gain(ks[16], (N_EVEN, SSD_WIDTH))
    even_w_out = nrm(ks[17], (N_EVEN, EVEN_MIX, D_MODEL), EVEN_MIX)
    odd_norm = gain(ks[18], (N_ODD, D_MODEL))
    odd_w_in = nrm(ks[19], (N_ODD, D_MODEL, ODD_IN), D_MODEL)
    odd_w_out = nrm(ks[20], (N_ODD, SB_WIDTH, D_MODEL), SB_WIDTH)
    final_norm = gain(ks[21], (D_MODEL,))
    return {'x': x, 'meta': meta, 'even_norm': even_norm, 'even_w_in': even_w_in,
            'lru_conv_w': lru_conv_w, 'lru_conv_b': lru_conv_b,
            'lru_w_a': lru_w_a, 'lru_b_a': lru_b_a, 'lru_w_x': lru_w_x, 'lru_b_x': lru_b_x,
            'lru_lambda': lru_lambda, 'ssd_conv_w': ssd_conv_w, 'ssd_conv_b': ssd_conv_b,
            'ssd_dt_bias': ssd_dt_bias, 'ssd_a_log': ssd_a_log, 'ssd_d': ssd_d,
            'ssd_norm': ssd_norm, 'even_w_out': even_w_out, 'odd_norm': odd_norm,
            'odd_w_in': odd_w_in, 'odd_w_out': odd_w_out, 'final_norm': final_norm}

def second_block(x, meta, even_norm, even_w_in, lru_conv_w, lru_conv_b, lru_w_a, lru_b_a,
              lru_w_x, lru_b_x, lru_lambda, ssd_conv_w, ssd_conv_b, ssd_dt_bias,
              ssd_a_log, ssd_d, ssd_norm, even_w_out, odd_norm, odd_w_in, odd_w_out,
              final_norm):
    bsz = x.shape[0]
    meta_b = jnp.broadcast_to(meta[None].astype(x.dtype), (bsz, N_META, D_MODEL))
    h = jnp.concatenate([meta_b, x], axis=1)
    for layer in range(DEPTH):
        j = layer // 2
        if layer % 2 == 0:
            h = rglru_ssd_layer(h, even_norm[j], even_w_in[j], lru_conv_w[j], lru_conv_b[j],
                                lru_w_a[j], lru_b_a[j], lru_w_x[j], lru_b_x[j], lru_lambda[j],
                                ssd_conv_w[j], ssd_conv_b[j], ssd_dt_bias[j], ssd_a_log[j],
                                ssd_d[j], ssd_norm[j], even_w_out[j])
        else:
            h = stick_breaking_layer(h, odd_norm[j], odd_w_in[j], odd_w_out[j])
    return rmsnorm(h, final_norm)[:, N_META:].astype(x.dtype)


def setup_inputs(seed=0):
    out = dict(first_inputs(seed))
    for name, value in second_inputs(seed + 1).items():
        if name != "x":
            out[name + "_2"] = value
    return out


def reference(
    x, c, ctx, c_ctx, w_mod, b_mod, g_pre, g_post, w_ffn_in, w_ffn_out, w_in, w_out, na_rpb,
    swa_sink, meta_2, even_norm_2, even_w_in_2, lru_conv_w_2, lru_conv_b_2, lru_w_a_2,
    lru_b_a_2, lru_w_x_2, lru_b_x_2, lru_lambda_2, ssd_conv_w_2, ssd_conv_b_2, ssd_dt_bias_2,
    ssd_a_log_2, ssd_d_2, ssd_norm_2, even_w_out_2, odd_norm_2, odd_w_in_2, odd_w_out_2,
    final_norm_2,
):
    x = first_block(
        x, c, ctx, c_ctx, w_mod, b_mod, g_pre, g_post, w_ffn_in, w_ffn_out, w_in, w_out, na_rpb,
        swa_sink,
    )
    return second_block(
        x, meta_2, even_norm_2, even_w_in_2, lru_conv_w_2, lru_conv_b_2, lru_w_a_2, lru_b_a_2,
        lru_w_x_2, lru_b_x_2, lru_lambda_2, ssd_conv_w_2, ssd_conv_b_2, ssd_dt_bias_2,
        ssd_a_log_2, ssd_d_2, ssd_norm_2, even_w_out_2, odd_norm_2, odd_w_in_2, odd_w_out_2,
        final_norm_2,
    )


_drawn_inputs = setup_inputs


def setup_inputs(seed=0):
    import zlib

    import numpy as np

    out = dict(_drawn_inputs(seed))
    spreads = {}
    factors = {'g_pre': 7.904,
     'g_post': 8.0,
     'na_rpb': 8.0,
     'swa_sink': 8.0,
     'lru_b_a_2': 25.487,
     'lru_b_x_2': 12.716,
     'ssd_d_2': 17.777,
     'odd_norm_2': 2.676,
     'ssd_conv_b_2': 3.334,
     'ssd_norm_2': 3.876}
    for name, (base, spread) in spreads.items():
        noise = np.random.default_rng([zlib.crc32(name.encode()), seed]).standard_normal(out[name].shape)
        drawn = base * np.exp(spread * noise) if base else spread * noise
        out[name] = __import__('jax').numpy.asarray(drawn.astype(out[name].dtype))
    for name, factor in factors.items():
        out[name] = (out[name] * factor).astype(out[name].dtype)
    return out
```

```python
from contextlib import ExitStack, contextmanager

import numpy as np

import concourse.bass as bass
from concourse import mybir

F32 = mybir.dt.float32
F32R = mybir.dt.float32r
ALU = mybir.AluOpType
ACT = mybir.ActivationFunctionType
AX_X = mybir.AxisListType.X

P = 128
D = 1024
DT = D // P
SEQ = 512
CTX = 256
META = 16
T1 = SEQ + CTX
T2 = META + SEQ
TOT = META + SEQ + CTX
DEPTH = 2
F_TILES = 22
F_PARTS = [(0, 8), (8, 8), (16, 6)]
N_MOD = 9
HD = 64
GRID_W = 64
NEG = -1e30
EPS = 1e-6
QSCALE = HD ** -0.5
HEADS = 16
XBC_TILES = 12
RPB_W = 2 * GRID_W - 1
PRIME = 4
MOD_CHUNKS = DEPTH * N_MOD * D // SEQ


def columns():
    widths = [
        ("ident", 128), ("ones", 128), ("na_mask", GRID_W), ("swa_mask", 384), ("rope_rot", 128),
        ("four_cos", 128), ("four_sin", 128), ("ssd_mask", 128), ("sb_mask", 128), ("sb_keep", 128),
        ("g_pre", 48), ("g_post", 48), ("b_mod", 144), ("sink", 12), ("cond", 16),
        ("even_norm", 8), ("lru_cw", 32), ("lru_cb", 8), ("lru_ba", 8), ("lru_bx", 8), ("lru_lam", 8),
        ("ssd_cw", 48), ("ssd_cb", 12), ("ssd_d", 8), ("ssd_norm", 8), ("odd_norm", 8), ("final_norm", 8),
        ("dt_bias", 1), ("a_log", 1),
    ]
    at, n = {}, 0
    for name, w in widths:
        at[name] = (n, w)
        n += w
    return at, n


COL, N_COL = columns()


class Chain:

    def __init__(self, eng, sem):
        self.eng, self.sem, self.n, self.off = eng, sem, 0, 0

    def __call__(self, ins):
        self.n += 1
        ins.then_inc(self.sem, 1)
        self.eng.wait_ge(self.sem, self.n + self.off)

    @contextmanager
    def loop(self, i, times, per):
        n = self.n
        self.off = i * per
        yield
        assert self.n == n + per
        self.n, self.off = n + per * times, 0


def build(nc, xT, ctxT, metaT, const, modw, wu, rpb, rope, four, four_c, gatew, out, stop=99):
    NU = wu.shape[0]
    BASE = 16512
    at = [BASE]

    def place(name, shape, dt, offset=None):
        size = 4 * int(np.prod(shape[1:]))
        if offset is None:
            offset = at[0]
            at[0] += (size + 31) // 32 * 32
        return nc.alloc_sbuf_tensor_at(name, shape, dt, offset=offset)

    XT = place("resid", [P, DT, TOT], F32)
    H = place("h_parts", [P, 2, DT, T1], F32R)
    a_arena = at[0]
    at[0] += 49664
    G = place("hidden_parts", [P, 2, DT, T1], F32R, a_arena)
    MODRING = place("mod_ring", [P, 3, DT, SEQ], F32, a_arena)
    QK = place("qk", [P, 10, T1], F32, a_arena)
    VT = place("v_tok", [P, 6, T1], F32, a_arena + 10 * T1 * 4)
    a_y = at[0]
    Y = place("y_acc", [P, DT, T1], F32)
    FC = place("four_dft", [P, 2, 4, SEQ], F32, a_y)
    FCC = place("four_dft_ctx", [P, 2, 2, CTX], F32, a_y + 2 * 4 * SEQ * 4)
    TB = place("na_bias", [P, 2, 16, GRID_W], F32, a_y)
    SB = place("scores", [P, 3, T1 + 8], F32, a_y + 8192)
    PT = place("probs_t", [P, 2, T1], F32, a_y + 8192 + 3 * (T1 + 8) * 4)
    RAW = place("w_raw", [P, 4, DT, P], F32)
    SPL = place("w_parts", [P, 2, 2, DT, P], F32R)
    a_t = at[0]
    at[0] += 20992
    TS = place("silu_gate", [P, 2, T1], F32, a_t + 6144)
    V = place("to_split", [P, 2, T1], F32, a_t)
    ACC = place("sq_sum", [P, T1], F32, a_t + 12288)
    SQ = place("squares", [P, 2, T1], F32, a_t + 6144)
    TN = place("normed", [P, 2, T1], F32, a_t + 6144)
    DG = place("rstd_diag", [P, T1], F32, a_t + 15360)
    FA = place("four_a", [P, 4, T1], F32, a_t + 6144)
    MROW = place("mod_rows", [P, 3, SEQ], F32, a_t)
    ROPE = place("rope_tab", [P, 2, SEQ], F32, a_y + 20480)
    RT = place("rope_tmp", [P, 2, SEQ], F32, a_t)
    K = place("const", [P, N_COL], F32)
    MODS = place("mods", [P, 144, 2], F32)
    ST = place("stats", [P, 4, 8], F32)
    SM = place("softmax_stats", [P, 3, 4], F32)
    LAM = place("lru_rates", [P, 8, 8], F32)
    PRM = place("primer", [P, 16], F32)
    assert at[0] <= 229344, at[0]
    a_h = BASE + DT * TOT * 4
    a_ht = a_h + 2 * DT * T2 * 4
    H2 = place("h2_parts", [P, 2, DT, T2], F32R, a_h)
    GWX = place("gate_wx", [P, 4, 2, 2, P], F32, a_ht)
    YA = place("lru_y_parts", [P, 2, DT, T2], F32R, a_arena)
    GWA = place("gate_wa", [P, 4, 2, 2, P], F32, a_arena + 2 * DT * T2 * 4)
    LX = place("lru_x", [P, DT, T2], F32, a_y)
    V2 = place("to_split2", [P, 2, T2], F32, a_t)
    PAD = place("conv_in", [P, 2, T2 + 8], F32, a_t + 6144)
    CV = place("conv_out", [P, 2, T2], F32, a_t + 10432)
    GR = place("gate_r", [P, 2, T2], F32, a_t + 6144)
    GI = place("gate_i", [P, 2, T2], F32, a_t + 10368)
    GA = place("gate_decay", [P, 2, T2], F32, a_t + 14592)
    GB = place("gate_sq", [P, T2], F32, a_t + 18816)
    TG = place("silu_g", [P, 2, T2], F32, a_t + 6144)
    TN2 = place("normed2", [P, 2, T2], F32, a_t + 6144)
    SQ2 = place("squares2", [P, 2, T2], F32, a_ht + 8192)
    Z = place("silu_z", [P, DT, T2], F32, a_arena)
    XS = place("ssd_x", [P, DT, T2], F32, a_arena + 16896)
    BC = place("ssd_bc", [P, 4, T2], F32, a_arena + 33792)
    CB = place("ssd_cb", [P, 1360], F32, a_arena + 42240)
    COLS = place("ssd_cols", [P, 3, 5, HEADS], F32, a_arena + 47680)
    XDT = place("ssd_xdt", [P, 5, D], F32, a_y)
    DTR = place("dt_rows", [P, 8, T2], F32, a_y)
    CUM = place("ssd_cum", [P, 1360], F32, a_t + 14656)
    EE = place("ssd_decay", [P, 2, T2], F32, a_t + 6144)
    WW = place("ssd_w", [P, 2, T2], F32, a_t + 10368)
    ACC2 = place("sq_sum2", [P, 2, T2], F32, a_ht)
    DG2 = place("rstd_diag2", [P, T2], F32, a_ht + 4224)
    KK = place("sb_k", [P, DT, T2], F32, a_arena)
    QQ = place("sb_q", [P, DT, SEQ], F32, a_arena + 16896)
    SG = place("sb_silu_g", [P, DT, SEQ], F32, a_arena + 33280)
    VV = place("sb_v", [P, 5, D], F32, a_y)
    V3 = place("to_split3", [P, 2, SEQ], F32, a_y + 20480)
    WA = place("sb_logw", [P, 3, T2], F32, a_t)
    WB = place("sb_sp", [P, 2, T2], F32, a_t + 6336)
    WC = place("sb_cum", [P, 2, T2 + 8], F32, a_t + 10560)
    WT = place("sb_wt", [P, 2, 640], F32, a_t + 14848)
    H3 = place("h3_parts", [P, 2, DT, SEQ], F32R, a_h)
    FIN = place("final", [P, DT, SEQ], F32, a_arena)

    PS = nc.alloc_psum_tensor("psum", [P, 4, 1024], F32)
    PSF = PS[:].rearrange("p a c -> p (a c)")

    def token_psum(u, nt):
        o = (u % 4) * 1024
        return PSF[:, o:o + nt * 2 * P].rearrange("p (t c) -> p t c", c=2 * P)

    def spans(T):
        return [(0, T2 // 2), (T2 // 2, T2)] if T == T2 else [(a, min(T, a + SEQ)) for a in range(0, T, SEQ)]

    def row2(t):
        return t.rearrange("p (a c) -> p a c", a=2)

    def twop(pair):
        return PS[:, pair].rearrange("p (a c) -> p a c", a=2)[:, :, 0:T2 // 2]

    def two(u):
        return twop(u % 4)

    def pad_row(j):
        return row2(PAD[:, j % 2, 3:3 + T2])

    PSO = {0: 0, SEQ: SEQ, T2 // 2: SEQ}
    sems = {}

    def sem(name):
        if name not in sems:
            sems[name] = nc.alloc_semaphore(name)
        return sems[name]

    const_in, x_in = sem("const_in"), sem("x_in")
    mod_in = [sem(f"mod_in{s}") for s in range(3)]
    mod_used = sem("mod_used")
    raw_in = [sem(f"raw_in{s}") for s in range(4)]
    w_hi, w_split, unit_done = sem("w_hi"), sem("w_split"), sem("unit_done")
    silu_ready, psum_read = sem("silu_ready"), sem("psum_read")
    v_ready, v_hi, v_split = sem("v_ready"), sem("v_hi"), sem("v_split")
    sq_ready, sq_added, resid_ready = sem("sq_ready"), sem("sq_added"), sem("resid_ready")
    tot_ready, ms_ready, root_ready, diag_ready, rb_ready = (
        sem("tot_ready"), sem("ms_ready"), sem("root_ready"), sem("diag_ready"), sem("rstd_ready"))
    dve_step, act_step = sem("dve_step"), sem("act_step")
    cact_ready, mod_row, mod_tr = sem("cact_ready"), sem("mod_row_read"), sem("mod_transposed")
    tab_in = sem("tab_in")
    tb_in = [sem("tb_in0"), sem("tb_in1")]
    rope_rot, rope_done = sem("rope_rot"), sem("rope_done")
    four_a_s, four_ev, four_b_s = sem("four_a"), sem("four_read"), sem("four_b")
    s_mm, s_ctx, s_max, s_exp, s_norm, s_tr, s_trc, s_pv = (
        sem("score_mm"), sem("score_ctx"), sem("score_max"), sem("score_exp"), sem("prob_ready"),
        sem("prob_tr"), sem("prob_tr_read"), sem("pv_done"))
    out_sem = sem("out_done")
    gate_w_in, pad_ready, conv_done, gate_mm, gate_read = (
        sem("gate_w_in"), sem("pad_ready"), sem("conv_done"), sem("gate_mm"), sem("gate_read"))
    lam_abs, lam_exp, decay_ready, mult_ready, mult_root, lru_h = (
        sem("lam_abs"), sem("lam_exp"), sem("decay_ready"), sem("mult_ready"), sem("mult_root"), sem("lru_h"))
    dt_abs, dt_exp, dt_rows, dt_cols, xbc_ready = (
        sem("dt_abs"), sem("dt_exp"), sem("dt_rows"), sem("dt_cols_mm"), sem("xbc_ready"))
    cols_read, xdt_mm, xdt_ready, cb_mm, cb_read = (
        sem("dt_cols_read"), sem("xdt_mm"), sem("xdt_ready"), sem("cb_mm"), sem("cb_read"))
    bc_mm, masked, e_ready, w_ready, ssd_y, y_read, gated = (
        sem("ssd_bc_mm"), sem("ssd_masked"), sem("ssd_decay_ready"), sem("ssd_w_ready"), sem("ssd_y"), sem("ssd_y_read"),
        sem("ssd_gated"))
    z_mm, relu_ready, ln_ready, logw_ready, weight_ready, wt_mm, wt_read, sb_pv = (
        sem("sb_z_mm"), sem("sb_relu"), sem("sb_ln"), sem("sb_logw"), sem("sb_weight"), sem("sb_tr"), sem("sb_tr_read"),
        sem("sb_pv"))
    abs_ready, final_ready = sem("sb_abs"), sem("final_ready")

    def col(name, i=0, n=1, rows=P):
        a, w = COL[name]
        assert i + n <= w
        return K[0:rows, a + i:a + i + n]

    def mod_col(l, m, k, c):
        j = l * 72 + m * 8 + k
        return MODS[:, j, c:c + 1]

    subs = []
    for l in range(DEPTH):
        subs.append(dict(kind="ffn", l=l, s=0, T=T1))
        subs.append(dict(kind="mix", l=l, s=1, T=T1 if l < DEPTH - 1 else SEQ))
        subs.append(dict(kind="ffn", l=l, s=2, T=T1 if l < DEPTH - 1 else SEQ))
    whole = stop > len(subs)
    subs = subs[:stop]
    n = dict(u=0, silu=PRIME, pr=PRIME, e=PRIME, q=0, sq=PRIME, xr=PRIME, att=PRIME, head=0, mix=0)
    for sub in subs:
        sub["in"] = dict(n)
        n["q"] += 2
        n["sq"] += 16
        n["xr"] += 8
        n["e"] += 8
        if sub["kind"] == "ffn":
            n["u"] += 68
            n["silu"] += 22
            n["e"] += 22
            n["pr"] += 24
        else:
            n["u"] += 24
            n["pr"] += 24
            n["e"] += 8
            n["att"] += 72 if sub["T"] == T1 else 48
            n["head"] += 6
            n["mix"] += 1
    end = n
    U2, E2, Q2, SQB, XR2, PR2, SI2 = (end[k] for k in ("u", "e", "q", "sq", "xr", "pr", "silu"))
    n_units = end["u"] + (93 if whole else 0) + 2
    SSD_TILES = [(128 * i, min(128 * i + 128, T2)) for i in range(5)]
    SSD_OFF = [0, 528, 928, 1200, 1344]
    def chunks(T):
        return [(0, SEQ, 0)] + ([(SEQ, T1, 1)] if T == T1 else [])

    def xt(m, T):
        return XT[:, m, META:META + T]

    def att_steps(sub):
        both = sub["T"] == T1
        steps = []
        for ot in range(6):
            na = ot < 3
            for half in range(2):
                rows = slice(half * HD, half * HD + HD)
                head = 2 * ot + half if na else (ot - 3) + 3 * half
                for t in range(6 if both else 4):
                    st = dict(ot=ot, half=half, rows=rows, t=t, na=na, head=head,
                              q=(ot if na else 6 + ot - 3), k=(3 + ot if na else 9),
                              vcol=(head * HD if na else 384 + half * HD),
                              sink=None if na else sub["l"] * 6 + head, last=half == 1 and t == (5 if both else 3),
                              first_of_head=t == 0)
                    if t >= 4:
                        st.update(lat=None, tt=[4, 5])
                    elif na:
                        st.update(lat=(0, SEQ), tt=[0, 1, 2, 3, 4, 5])
                    else:
                        b0, b1 = max(0, t - 1), min(3, t + 1)
                        st.update(lat=(b0 * P, (b1 + 1) * P), tt=list(range(b0, b1 + 1)) + [4, 5],
                                  mask=(b0 - t + 1) * P)
                    steps.append(st)
        return steps

    with nc.Block() as block:

        @block.sync
        def _(sp):
            sp.dma_start(K[:], const).then_inc(const_in, 16)
            sp.dma_start(XT[:, :, META:META + SEQ], xT).then_inc(x_in, 16)
            sp.dma_start(XT[:, :, META + SEQ:TOT], ctxT).then_inc(x_in, 16)
            sp.dma_start(XT[:, :, 0:META], metaT).then_inc(x_in, 16)

            def mod_load(i, s):
                sp.dma_start(MODRING[:, s].rearrange("p k m -> p (k m)"),
                             modw[bass.ds(i * 3 + s, 1)].rearrange("a p n -> p (a n)")).then_inc(mod_in[s], 16)

            for s in range(3):
                mod_load(0, s)
            with sp.Fori(1, MOD_CHUNKS // 3) as i:
                for s in range(3):
                    sp.wait_ge(mod_used, i * 3 + (s - 2))
                    mod_load(i, s)

            def w_load(u, s):
                sp.dma_start(RAW[:, s].rearrange("p k m -> p (k m)"),
                             wu[bass.ds(u, 1)].rearrange("a p n -> p (a n)")).then_inc(raw_in[s], 16)

            for u in range(4):
                w_load(u, u)
            loops = n_units // 4
            with sp.Fori(1, loops) as i:
                for s in range(4):
                    sp.wait_ge(w_split, i * 4 + (s - 3))
                    w_load(i * 4 + s, s)
            for u in range(loops * 4, n_units):
                sp.wait_ge(w_split, u - 3)
                w_load(u, u % 4)

        @block.gpsimd
        def _(pool):
            def low_part(u, s, i=0):
                pool.wait_ge(w_hi, u + 1)
                pool.tensor_tensor(SPL[:, s % 2, 1], RAW[:, s], SPL[:, s % 2, 0].bitcast(F32),
                                   ALU.subtract).then_inc(w_split, 1)

            loops = n_units // 4
            with pool.Fori(0, loops) as i:
                for s in range(4):
                    low_part(i * 4 + s, s)
            for u in range(loops * 4, n_units):
                low_part(u, u % 4)

        @block.scalar
        def _(act):
            step = Chain(act, act_step)

            def high_part(u0, i, j):
                u = u0 + j
                if u >= n_units:
                    return
                act.wait_ge(raw_in[u % 4], (i + (u // 4 + 1)) * 16)
                if u >= 2:
                    act.wait_ge(unit_done, i * 4 + (u - 1))
                act.activation(SPL[:, u % 2, 0], RAW[:, u % 4], ACT.Copy).then_inc(w_hi, 1)

            def split_high(dst, src, e):
                act.wait_ge(v_ready, e + 1)
                act.activation(dst, src, ACT.Copy).then_inc(v_hi, 1)

            def squares(src, T, sq, wait=None):
                for m in range(DT):
                    if wait:
                        act.wait_ge(wait[0], wait[1] + m)
                    act.wait_ge(sq_added, sq + m - 1)
                    act.activation(SQ[:, m % 2, 0:T], src(m), ACT.Square).then_inc(sq_ready, 1)

            def root(q):
                act.wait_ge(ms_ready, q + 1)
                act.activation(ST[:, 1, :], ST[:, 0, :], ACT.Sqrt).then_inc(root_ready, 1)

            def pre_apply(sub, e0, T):
                for k in range(DT):
                    split_high(H[:, 0, k, 0:T], V[:, k % 2, 0:T], e0 + k)

            def ffn(sub, b):
                T = sub["T"]
                u, e, silu, pr = b["u"], b["e"] + 8, b["silu"], b["pr"]
                for part, (f0, nf) in enumerate(F_PARTS):
                    with act.Fori(0, nf // 2) as i:
                        for j in range(4):
                            act.wait_ge(unit_done, i * 4 + (u + j + 1))
                            high_part(u, i, j + 2)
                            if j < 2:
                                act.wait_ge(v_ready, i * 2 + (e + j - 1))
                                act.activation(TS[:, j, 0:T], PS[:, (u + j) % 4, 0:T], ACT.Silu).then_inc(silu_ready, 1)
                            else:
                                split_high(G[:, 0, bass.ds(i * 2 + (j - 2), 1), 0:T].rearrange("p a t -> p (a t)"),
                                           V[:, j - 2, 0:T], i * 2 + (e + j - 2))
                    u += 2 * nf
                    e += nf
                    silu += nf
                    out_units(sub, u, pr, b["sq"] + 8, T, accumulate=part == len(F_PARTS) - 1)
                    u += 8
                    pr += 8

            def out_units(sub, u, pr, sq, T, accumulate):
                with act.Fori(0, 2) as i:
                    for j in range(4):
                        act.wait_ge(unit_done, i * 4 + (u + j + 1))
                        high_part(u, i, j + 2)
                        if accumulate:
                            act.wait_ge(psum_read, i * 4 + (pr + j + 1))
                            act.wait_ge(sq_added, i * 4 + (sq + j - 1))
                            act.activation(SQ[:, j % 2, 0:T], Y[:, bass.ds(i * 4 + j, 1), 0:T].rearrange("p a t -> p (a t)"),
                                           ACT.Square).then_inc(sq_ready, 1)

            def mix(sub, b):
                T, l = sub["T"], sub["l"]
                u, e, a0, h0, mx = b["u"], b["e"] + 8, b["att"], b["head"], b["mix"]
                act.wait_ge(resid_ready, b["xr"])
                act.wait_ge(v_split, b["e"] + 8)
                act.dma_start(FC[:], four).then_inc(tab_in, 16)
                act.dma_start(FCC[:], four_c).then_inc(tab_in, 16)
                act.dma_start(ROPE[:], rope).then_inc(tab_in, 16)
                for j in range(16):
                    act.wait_ge(unit_done, u + j + 1)
                    high_part(u, 0, j + 2)
                for r in range(4):
                    act.wait_ge(four_a_s, 4 * mx + r + 1)
                    act.activation(FA[:, r, 0:T], PS[:, r, 0:T], ACT.Copy).then_inc(four_ev, 1)
                for r in range(2):
                    split_high(H[:, 0, 6 + r, 0:T], V[:, r, 0:T], e + r)
                e += 2
                steps = att_steps(sub)

                def bias_load(h):
                    for hf in range(2):
                        act.dma_start(TB[hf * HD:hf * HD + HD, h % 2, 1:15, :],
                                      rpb[l * 6 + h, :, 1 - hf:15 - hf]).then_inc(tb_in[h % 2], 16)

                act.wait_ge(four_b_s, 2 * (mx + 1))
                act.wait_ge(four_ev, 4 * (mx + 1))
                bias_load(0)
                bias_load(1)
                N = len(steps)
                for i in range(-1, N + 1):
                    if i + 1 < N:
                        st, a = steps[i + 1], a0 + i + 1
                        w = (st["lat"][1] - st["lat"][0]) if st["lat"] else 0
                        act.wait_ge(s_mm, a + 1)
                        act.wait_ge(s_tr, a - 2)
                        act.activation(SB[:, a % 3, 1 + w:1 + w + CTX], PS[:, a % 2, SEQ:SEQ + CTX], ACT.Copy,
                                       scale=QSCALE).then_inc(s_ctx, 1)
                    if 0 <= i < N:
                        st, a = steps[i], a0 + i
                        w = ((st["lat"][1] - st["lat"][0]) if st["lat"] else 0) + CTX
                        lo = 0 if st["sink"] is not None else 1
                        act.wait_ge(s_max, a + 1)
                        act.activation(SB[:, a % 3, lo:1 + w], SB[:, a % 3, lo:1 + w], ACT.Exp,
                                       bias=SM[:, a % 3, 1:2], accum_out=SM[:, a % 3, 2:3]).then_inc(s_exp, 1)
                        if st["na"] and st["first_of_head"] and 1 <= st["head"] <= 4:
                            act.wait_ge(s_max, a)
                            bias_load(st["head"] + 1)
                    if 0 <= i - 1 < N:
                        st, a = steps[i - 1], a0 + i - 1
                        w = len(st["tt"]) * P
                        act.wait_ge(s_tr, a + 1)
                        act.wait_ge(s_pv, a - 1)
                        act.activation(PT[:, a % 2, 0:w], PS[:, 2, 0:w], ACT.Copy).then_inc(s_trc, 1)
                        if st["last"]:
                            split_high(H[:, 0, st["ot"], 0:T], V[:, e % 2, 0:T], e)
                            e += 1
                u += 16
                out_units(sub, u, b["pr"] + 16, b["sq"] + 8, T, accumulate=True)

            def unit_steps(u, n):
                for j in range(n):
                    act.wait_ge(unit_done, u + j + 1)
                    high_part(u, 0, j + 2)
                    yield j

            def even_layer():
                u, e = U2, E2
                root(Q2)
                act.wait_ge(diag_ready, Q2 + 1)
                act.dma_start(GWA[:], gatew[:, 0]).then_inc(gate_w_in, 16)
                act.dma_start(GWX[:], gatew[:, 1]).then_inc(gate_w_in, 16)
                act.wait_ge(lam_abs, 1)
                act.activation(LAM[:, 1], LAM[:, 0], ACT.Exp, scale=-1.0).then_inc(lam_exp, 1)
                for k in range(DT):
                    split_high(H2[:, 0, k], V2[:, k % 2], e + k)
                e += 8
                for j in unit_steps(u, 8):
                    if j >= 2:
                        act.wait_ge(conv_done, j - 1)
                    act.activation(pad_row(j), two(u + j), ACT.Copy).then_inc(pad_ready, 1)
                u += 8
                act.wait_ge(conv_done, 8)
                for g in range(4):
                    for t in range(2):
                        m = 2 * g + t
                        act.wait_ge(gate_mm, 2 * m + 2)
                        if g > 0:
                            act.wait_ge(lru_h, m - 1)
                        for x, (dst, bias) in enumerate(((GR, "lru_ba"), (GI, "lru_bx"))):
                            act.activation(row2(dst[:, t]), twop(2 * (m % 2) + x), ACT.Sigmoid, bias=col(bias, m)).then_inc(gate_read, 1)
                    for t in range(2):
                        m = 2 * g + t
                        act.wait_ge(gate_read, 2 * m + 1)
                        act.activation(GA[:, t], GR[:, t], ACT.Exp, scale=LAM[:, 2, m:m + 1]).then_inc(act_step, 1)
                        act.wait_ge(act_step, m + 1)
                        act.activation(GR[:, t], GR[:, t], ACT.Tanh, scale=LAM[:, 3, m:m + 1]).then_inc(decay_ready, 1)
                    for t in range(2):
                        m = 2 * g + t
                        act.wait_ge(mult_ready, m + 1)
                        act.activation(GR[:, t], GR[:, t], ACT.Sqrt).then_inc(mult_root, 1)
                act.wait_ge(lru_h, 8)
                for j in unit_steps(u, 8):
                    act.wait_ge(v_ready, e + j - 1)
                    act.activation(row2(TG[:, j % 2]), two(u + j), ACT.Silu).then_inc(silu_ready, 1)
                    if j > 0:
                        split_high(YA[:, 0, j - 1], V2[:, (j - 1) % 2], e + j - 1)
                split_high(YA[:, 0, 7], V2[:, 1], e + 7)
                u += 8
                e += 8
                for j in unit_steps(u, 8):
                    pass
                u += 8
                for j in unit_steps(u, 1):
                    pass
                act.wait_ge(dt_abs, 1)
                act.activation(DTR[0:HEADS, 2], DTR[0:HEADS, 1], ACT.Exp, scale=-1.0).then_inc(dt_exp, 1)
                act.activation(LAM[0:HEADS, 0, 0:1], col("a_log", 0, 1, HEADS), ACT.Exp).then_inc(dt_exp, 1)
                u += 1
                for j in unit_steps(u, 12):
                    act.wait_ge(conv_done, 8 + j - 1)
                    act.activation(pad_row(j), two(u + j), ACT.Copy).then_inc(pad_ready, 1)
                    if j > 0:
                        xbc_silu(j - 1)
                xbc_silu(11)
                u += 12
                for j in unit_steps(u, 8):
                    act.activation(row2(Z[:, j]), two(u + j), ACT.Silu).then_inc(silu_ready, 1)
                u += 8
                for g in range(2):
                    for i, (a, z) in enumerate(SSD_TILES):
                        c = 5 * g + i
                        act.wait_ge(cb_mm, c + 1)
                        if g > 0:
                            act.wait_ge(w_ready, 40)
                        act.activation(CB[0:z - a, SSD_OFF[i]:SSD_OFF[i] + T2 - a], PS[0:z - a, c % 2, 0:T2 - a],
                                       ACT.Copy).then_inc(cb_read, 1)
                    for h in range(8 * g, 8 * g + 8):
                        for i, (a, z) in enumerate(SSD_TILES):
                            s_, w, R = 5 * h + i, z - a, z - a
                            act.wait_ge(bc_mm, s_ + 1)
                            act.wait_ge(masked, s_ + 1)
                            if s_ >= 2:
                                act.wait_ge(w_ready, s_ - 1)
                            if z < T2:
                                act.activation(EE[0:R, s_ % 2, w:T2 - a], PS[0:R, s_ % 2, w:T2 - a], ACT.Exp,
                                               bias=COLS[0:R, 1, i, h:h + 1])
                            act.activation(EE[0:R, s_ % 2, 0:w], EE[0:R, s_ % 2, 0:w], ACT.Exp,
                                           bias=COLS[0:R, 0, i, h:h + 1]).then_inc(e_ready, 1)
                        if h % 2:
                            m = h // 2
                            act.wait_ge(gated, m + 1)
                            act.wait_ge(sq_added, SQB + 8 + m - 1)
                            act.activation(SQ2[:, m % 2], XS[:, m], ACT.Square).then_inc(sq_ready, 1)
                root(Q2 + 1)
                root(Q2 + 2)
                for k in range(DT):
                    split_high(H2[:, 0, k], V2[:, k % 2], e + k)
                for j in unit_steps(u, 8):
                    act.wait_ge(resid_ready, XR2 + j + 1)
                    act.wait_ge(sq_added, SQB + 16 + j - 1)
                    act.activation(SQ2[:, j % 2], XT[:, j, 0:T2], ACT.Square).then_inc(sq_ready, 1)

            def xbc_silu(j):
                act.wait_ge(conv_done, 8 + j + 1)
                dst = XS[:, j] if j < 8 else BC[:, j - 8]
                act.activation(dst, CV[:, j % 2], ACT.Silu).then_inc(xbc_ready, 1)

            def odd_layer():
                u, e = U2 + 53, E2 + 24
                root(Q2 + 3)
                for k in range(DT):
                    split_high(H2[:, 0, k], V2[:, k % 2], e + k)
                e += 8
                for j in unit_steps(u, 24):
                    pass
                for j in unit_steps(u + 24, 8):
                    act.activation(SG[:, j], PS[:, (u + 24 + j) % 4, 0:SEQ], ACT.Silu).then_inc(silu_ready, 1)
                act.preload_act_table_set("natural_log_exp_and_others")
                for i in range(-2, 64):
                    if i + 2 < 64:
                        a = i + 2
                        x = META + P * (a % 4 + 1)
                        b_ = WB[:, a % 2, 0:x]
                        act.wait_ge(z_mm, a + 1)
                        if a >= 2:
                            act.wait_ge(logw_ready, a - 1)
                        act.activation(b_, PS[:, a % 2, 0:x], ACT.Abs, scale=QSCALE).then_inc(abs_ready, 1)
                        act.wait_ge(abs_ready, a + 1)
                        act.activation(b_, b_, ACT.Exp, scale=-1.0).then_inc(act_step, 1)
                        act.wait_ge(act_step, 8 + a + 1)
                        act.activation(b_, b_, ACT.Ln, bias=1.0).then_inc(ln_ready, 1)
                    if i >= 0:
                        x = META + P * (i % 4 + 1)
                        act.wait_ge(logw_ready, i + 1)
                        act.activation(WA[:, i % 3, 0:x], WA[:, i % 3, 0:x], ACT.Exp, bias=SM[:, i % 3, 1:2]).then_inc(weight_ready, 1)
                    if i >= 8 and i % 8 == 1:
                        m = i // 8 - 1
                        split_high(H3[:, 0, m], V3[:, m % 2], e + m)
                split_high(H3[:, 0, 7], V3[:, 1], e + 7)
                u += 32
                for j in unit_steps(u, 8):
                    act.wait_ge(resid_ready, XR2 + 8 + j + 1)
                    act.wait_ge(sq_added, SQB + 24 + j - 1)
                    act.activation(SQ2[:, j % 2, 0:SEQ], XT[:, j, META:T2], ACT.Square).then_inc(sq_ready, 1)
                root(Q2 + 4)

            act.wait_ge(const_in, 16)
            act.activation(PRM[:, 13:14], col("ones"), ACT.Copy).then_inc(pad_ready, PRIME)
            for i, s in enumerate((silu_ready, v_hi, sq_ready)):
                act.activation(PRM[:, i:i + 1], col("ones"), ACT.Copy).then_inc(s, PRIME)
            act.activation(PRM[:, 12:13], col("ones"), ACT.Copy).then_inc(s_exp, PRIME)
            act.activation(PRM[:, 3:4], col("ones"), ACT.Copy).then_inc(s_ctx, PRIME)
            act.activation(PRM[:, 4:5], col("ones"), ACT.Copy).then_inc(s_trc, PRIME)
            act.activation(col("cond", 0, 16), col("cond", 0, 16), ACT.Silu).then_inc(cact_ready, 1)
            act.wait_ge(x_in, 48)
            for idx, sub in enumerate(subs):
                b = sub["in"]
                T = sub["T"]
                if idx == 0:
                    squares(lambda m: xt(m, T1), T1, b["sq"])
                    high_part(0, 0, 0)
                    high_part(0, 0, 1)
                root(b["q"])
                pre_apply(sub, b["e"], T1 if sub["kind"] == "mix" else T)
                if sub["kind"] == "ffn":
                    ffn(sub, b)
                else:
                    mix(sub, b)
                root(b["q"] + 1)
                if idx == len(subs) - 1 and whole:
                    squares(lambda m: XT[:, m, 0:T2], T2, b["sq"] + 16, wait=(resid_ready, b["xr"] + 1))
                else:
                    squares(lambda m: xt(m, T), T, b["sq"] + 16, wait=(resid_ready, b["xr"] + 1))
            if whole:
                even_layer()
                odd_layer()

        @block.vector
        def _(dve):
            step = Chain(dve, dve_step)

            def add_squares(T, sq):
                for m in range(DT):
                    add_square(T, sq + m, m == 0)

            def add_square(T, sq, first):
                dve.wait_ge(sq_ready, sq + 1)
                dve.wait_ge(sq_added, sq)
                if first:
                    dve.tensor_copy(ACC[:, 0:T], SQ[:, 0, 0:T]).then_inc(sq_added, 1)
                else:
                    dve.tensor_tensor(ACC[:, 0:T], ACC[:, 0:T], SQ[:, (sq - PRIME) % 2, 0:T], ALU.add).then_inc(sq_added, 1)

            def rstd(q, un, T, width=D, DG=DG):
                R, nt = (P, T // P) if T % P == 0 else (88, 6)
                dve.wait_ge(tot_ready, q + 1)
                dve.tensor_scalar(ST[0:R, 0, 0:nt], PS[0:R, (un + 2) % 4, 0:nt], 1.0 / width, EPS,
                                  ALU.mult, ALU.add).then_inc(ms_ready, 1)
                dve.wait_ge(root_ready, q + 1)
                step(dve.reciprocal(ST[0:R, 2, 0:nt], ST[0:R, 1, 0:nt]))
                dve.tensor_tensor(DG[0:R, 0:R * nt].rearrange("p (j c) -> p j c", j=nt),
                                  col("ident", 0, R, R).unsqueeze(1).broadcast_to([R, nt, R]),
                                  ST[0:R, 2, 0:nt].unsqueeze(2).broadcast_to([R, nt, R]), ALU.mult).then_inc(diag_ready, 1)

            def low_split(dst, src, hi, e):
                dve.wait_ge(v_hi, e + 1)
                dve.wait_ge(v_ready, e + 1)
                dve.tensor_tensor(dst, src, hi.bitcast(F32), ALU.subtract).then_inc(v_split, 1)

            def v_free(e):
                dve.wait_ge(v_hi, e - 1)
                dve.wait_ge(v_split, e - 1)

            def pre(sub, b, un):
                T, l, s, e = (T1 if sub["kind"] == "mix" else sub["T"]), sub["l"], sub["s"], b["e"]
                rstd(b["q"], un, T)
                dve.wait_ge(rb_ready, b["q"] + 1)
                for k in range(DT + 1):
                    if k < DT:
                        v_free(e + k)
                        step(dve.tensor_tensor(TN[:, k % 2, 0:T], xt(k, T), PS[:, (un + 3) % 4, 0:T], ALU.mult))
                        for a, z, c in chunks(T):
                            ins = dve.tensor_scalar(V[:, k % 2, a:z], TN[:, k % 2, a:z], mod_col(l, 3 * s + 1, k, c),
                                                    mod_col(l, 3 * s, k, c), ALU.mult, ALU.add)
                        ins.then_inc(v_ready, 1)
                    if k > 0:
                        low_split(H[:, 1, k - 1, 0:T], V[:, (k - 1) % 2, 0:T], H[:, 0, k - 1, 0:T], e + k - 1)

            def post(sub, b, un):
                T, l, s, q = sub["T"], sub["l"], sub["s"], b["q"] + 1
                rstd(q, un, T)
                dve.wait_ge(rb_ready, q + 1)
                for m in range(DT + 1):
                    if m < DT:
                        step(dve.tensor_tensor(Y[:, m, 0:T], Y[:, m, 0:T], PS[:, (un + 3) % 4, 0:T], ALU.mult))
                        for a, z, c in chunks(T):
                            ins = dve.scalar_tensor_tensor(XT[:, m, META + a:META + z], Y[:, m, a:z],
                                                           mod_col(l, 3 * s + 2, m, c), XT[:, m, META + a:META + z],
                                                           ALU.mult, ALU.add)
                        ins.then_inc(resid_ready, 1)
                    if m > 0:
                        if sub is subs[-1] and whole:
                            add_square(T2, b["sq"] + 16 + m - 1, m == 1)
                        else:
                            add_square(T, b["sq"] + 16 + m - 1, m == 1)

            def out_units(sub, u, pr, sq, T, first, accumulate):
                if accumulate:
                    step(dve.memset(ACC[:, 0:T], 0.0))
                dve.wait_ge(psum_read, pr)
                with dve.Fori(0, 2) as i:
                    for j in range(4):
                        y = Y[:, bass.ds(i * 4 + j, 1), 0:T].rearrange("p a t -> p (a t)")
                        ps = PS[:, (u + j) % 4, 0:T]
                        dve.wait_ge(unit_done, i * 4 + (u + j + 1))
                        if first:
                            dve.tensor_copy(y, ps).then_inc(psum_read, 1)
                        else:
                            dve.tensor_tensor(y, y, ps, ALU.add).then_inc(psum_read, 1)
                        if accumulate:
                            dve.wait_ge(sq_ready, i * 4 + (sq + j + 1))
                            dve.wait_ge(sq_added, i * 4 + (sq + j))
                            dve.tensor_tensor(ACC[:, 0:T], ACC[:, 0:T], SQ[:, j % 2, 0:T], ALU.add).then_inc(sq_added, 1)

            def ffn(sub, b):
                T = sub["T"]
                u, e, silu, pr = b["u"], b["e"] + 8, b["silu"], b["pr"]
                for part, (f0, nf) in enumerate(F_PARTS):
                    with dve.Fori(0, nf // 2) as i:
                        for j in range(2):
                            dve.wait_ge(unit_done, i * 4 + (u + j + 3))
                            dve.wait_ge(silu_ready, i * 2 + (silu + j + 1))
                            dve.wait_ge(v_hi, i * 2 + (e + j - 1))
                            dve.wait_ge(v_split, i * 2 + (e + j - 1))
                            dve.tensor_tensor(V[:, j, 0:T], TS[:, j, 0:T], PS[:, (u + j + 2) % 4, 0:T],
                                              ALU.mult).then_inc(v_ready, 1)
                            g = [G[:, x, bass.ds(i * 2 + j, 1), 0:T].rearrange("p a t -> p (a t)") for x in range(2)]
                            low_split(g[1], V[:, j, 0:T], g[0], i * 2 + (e + j))
                    u += 2 * nf
                    e += nf
                    silu += nf
                    out_units(sub, u, pr, b["sq"] + 8, T, first=part == 0, accumulate=part == len(F_PARTS) - 1)
                    u += 8
                    pr += 8

            def mix(sub, b):
                T, l = sub["T"], sub["l"]
                u, e, a0, mx = b["u"], b["e"] + 8, b["att"], b["mix"]
                for j in range(10):
                    dve.wait_ge(unit_done, u + j + 1)
                    Tj = T if j in (0, 1, 2, 6, 7, 8) else T1
                    dve.tensor_copy(QK[:, j, 0:Tj], PS[:, (u + j) % 4, 0:Tj]).then_inc(psum_read, 1)
                for j in range(10, 16, 2):
                    dve.wait_ge(unit_done, u + j + 2)
                    nt = (T if j >= 14 else T1) // P
                    dve.tensor_copy(VT[:, 0:nt, (j - 10) * P:(j - 8) * P], token_psum(u + j, nt)).then_inc(psum_read, 2)
                dve.wait_ge(tab_in, 48 * (mx + 1))
                dve.wait_ge(psum_read, b["pr"] + 16)
                for r in range(4):
                    dve.wait_ge(rope_rot, 4 * mx + r + 1)
                    qk = QK[:, 6 + r, 0:SEQ]
                    dve.tensor_tensor(RT[:, 0], PS[:, r, 0:SEQ], ROPE[:, 1], ALU.mult)
                    step(dve.tensor_tensor(RT[:, 1], qk, ROPE[:, 0], ALU.mult))
                    dve.tensor_tensor(qk, RT[:, 0], RT[:, 1], ALU.add).then_inc(rope_done, 1)
                    dve.wait_ge(rope_done, 4 * mx + r + 1)
                for r in range(2):
                    dve.wait_ge(four_b_s, 2 * mx + r + 1)
                    v_free(e + r)
                    dve.tensor_copy(V[:, r, 0:T], PS[:, r, 0:T]).then_inc(v_ready, 1)
                    low_split(H[:, 1, 6 + r, 0:T], V[:, r, 0:T], H[:, 0, 6 + r, 0:T], e + r)
                e += 2
                steps = att_steps(sub)
                N = len(steps)
                for i in range(-1, N + 1):
                    if i + 1 < N:
                        st, a = steps[i + 1], a0 + i + 1
                        sb = SB[:, a % 3]
                        w = 0
                        if st["na"] and st["first_of_head"]:
                            h = st["head"]
                            dve.wait_ge(tb_in[h % 2], 32 * (3 * mx + h // 2 + 1))
                            tbh = TB[:, h % 2, 1:15, :]
                            step(dve.tensor_tensor(tbh, tbh, col("na_mask", 0, GRID_W).unsqueeze(1).broadcast_to(
                                [P, 14, GRID_W]), ALU.add))
                        dve.wait_ge(s_mm, a + 1)
                        dve.wait_ge(s_tr, a - 2)
                        dve.wait_ge(s_norm, a - 2)
                        lo = 1
                        if st["sink"] is not None:
                            lo = 0
                            ins = dve.tensor_copy(sb[:, 0:1], col("sink", st["sink"]))
                        if st["lat"]:
                            w = st["lat"][1] - st["lat"][0]
                            if st["na"]:
                                d0 = 7 - 2 * st["t"]
                                bias = TB[:, st["head"] % 2, d0:d0 + 8, :].rearrange("p a c -> p (a c)")
                            else:
                                bias = col("swa_mask", st["mask"], w)
                            ins = dve.scalar_tensor_tensor(sb[:, 1:1 + w], PS[:, a % 2, 0:w], QSCALE, bias, ALU.mult, ALU.add)
                        if st["lat"] or st["sink"] is not None:
                            step(ins)
                        dve.wait_ge(s_ctx, a + 1)
                        step(dve.reduce_max(SM[:, a % 3, 0:1], sb[:, lo:1 + w + CTX], AX_X))
                        dve.tensor_scalar(SM[:, a % 3, 1:2], SM[:, a % 3, 0:1], -1.0, None, ALU.mult).then_inc(s_max, 1)
                    if 0 <= i < N:
                        st, a = steps[i], a0 + i
                        w = ((st["lat"][1] - st["lat"][0]) if st["lat"] else 0) + CTX
                        sb = SB[:, a % 3, 1:1 + w]
                        dve.wait_ge(s_exp, a + 1)
                        step(dve.reciprocal(SM[:, a % 3, 3:4], SM[:, a % 3, 2:3]))
                        dve.tensor_scalar(sb, sb, SM[:, a % 3, 3:4], None, ALU.mult).then_inc(s_norm, 1)
                    if 0 <= i - 1 < N and steps[i - 1]["last"]:
                        st, a = steps[i - 1], a0 + i - 1
                        dve.wait_ge(s_pv, a + 1)
                        v_free(e)
                        dve.tensor_copy(V[:, e % 2, 0:T], PS[:, 3, 0:T]).then_inc(v_ready, 1)
                        low_split(H[:, 1, st["ot"], 0:T], V[:, e % 2, 0:T], H[:, 0, st["ot"], 0:T], e)
                        e += 1
                out_units(sub, u + 16, b["pr"] + 16, b["sq"] + 8, T, first=True, accumulate=True)

            def pre_plain(q, un, T, gain, e):
                rstd(q, un, T)
                dve.wait_ge(rb_ready, q + 1)
                for k in range(DT + 1):
                    if k < DT:
                        v_free(e + k)
                        step(dve.tensor_tensor(TN2[:, k % 2], XT[:, k, 0:T2], PS[:, (un + 3) % 4, 0:T2], ALU.mult))
                        dve.tensor_scalar(V2[:, k % 2], TN2[:, k % 2], col(gain, k), None, ALU.mult).then_inc(v_ready, 1)
                    if k > 0:
                        low_split(H2[:, 1, k - 1], V2[:, (k - 1) % 2], H2[:, 0, k - 1], e + k - 1)

            def softplus(x, ax, ex, s_, s2, p_, exp_sem, n_):
                dve.wait_ge(exp_sem, n_)
                step(dve.tensor_scalar(ax, ex, 2.0, None, ALU.add))
                step(dve.reciprocal(s_, ax))
                step(dve.tensor_tensor(s_, s_, ex, ALU.mult))
                step(dve.tensor_tensor(s2, s_, s_, ALU.mult))
                step(dve.tensor_scalar(p_, s2, 1.0 / 15, None, ALU.mult))
                for n in (13, 11, 9, 7, 5, 3):
                    step(dve.scalar_tensor_tensor(p_, p_, 1.0 / n, s2, ALU.add, ALU.mult))
                step(dve.scalar_tensor_tensor(p_, p_, 1.0, s_, ALU.add, ALU.mult))
                step(dve.tensor_scalar(x, x, 0.0, None, ALU.max))
                step(dve.scalar_tensor_tensor(x, p_, 2.0, x, ALU.mult, ALU.add))

            def conv(dst, j, c, cw, cb, m):
                dve.wait_ge(pad_ready, PRIME + c + 1)
                row = PAD[:, j % 2]
                step(dve.tensor_scalar(dst, row[:, 0:T2], cw(m, 0), cb(m), ALU.mult, ALU.add))
                for tap in range(1, 4):
                    ins = dve.scalar_tensor_tensor(dst, row[:, tap:tap + T2], cw(m, tap), dst, ALU.mult, ALU.add)
                    if tap < 3:
                        step(ins)
                ins.then_inc(conv_done, 1)
                dve.wait_ge(conv_done, c + 1)

            def even_layer():
                u, e, pr = U2, E2, PR2
                step(dve.tensor_scalar(LAM[:, 4], col("lru_lam", 0, 8), -1.0, None, ALU.mult))
                dve.scalar_tensor_tensor(LAM[:, 0], LAM[:, 4], -1.0, LAM[:, 4], ALU.mult, ALU.max).then_inc(lam_abs, 1)
                pre_plain(Q2, u, T2, "even_norm", e)
                e += 8
                dve.wait_ge(lam_abs, 1)
                softplus(LAM[:, 4], LAM[:, 0], LAM[:, 1], LAM[:, 5], LAM[:, 6], LAM[:, 7], lam_exp, 1)
                step(dve.tensor_scalar(LAM[:, 2], LAM[:, 4], -8.0, None, ALU.mult))
                step(dve.tensor_scalar(LAM[:, 3], LAM[:, 4], 8.0, None, ALU.mult))
                dve.wait_ge(v_split, e)
                step(dve.memset(PAD[:, :, 0:3], 0.0))
                for j in range(8):
                    conv(LX[:, j], j, j, lambda m, t: col("lru_cw", t * 8 + m), lambda m: col("lru_cb", m), j)
                for g in range(4):
                    for t in range(2):
                        m = 2 * g + t
                        dve.wait_ge(decay_ready, m + 1)
                        step(dve.tensor_tensor(GB[:], GA[:, t], GA[:, t], ALU.mult))
                        dve.scalar_tensor_tensor(GR[:, t], GB[:], 1.0, GR[:, t], ALU.add, ALU.mult).then_inc(mult_ready, 1)
                        dve.wait_ge(mult_ready, m + 1)
                    dve.wait_ge(gate_mm, 4 * g + 4)
                    for t in range(2):
                        m = 2 * g + t
                        step(dve.tensor_tensor(GI[:, t], GI[:, t], LX[:, m], ALU.mult))
                        dve.wait_ge(mult_root, m + 1)
                        step(dve.tensor_tensor(GI[:, t], GI[:, t], GR[:, t], ALU.mult))
                        dve.tensor_tensor_scan(LX[:, m], GA[:, t], GI[:, t], 0.0, ALU.mult, ALU.add).then_inc(lru_h, 1)
                dve.wait_ge(lru_h, 8)
                for j in range(9):
                    if j < 8:
                        dve.wait_ge(silu_ready, SI2 + j + 1)
                        v_free(e + j)
                        dve.tensor_tensor(V2[:, j % 2], TG[:, j % 2], LX[:, j], ALU.mult).then_inc(v_ready, 1)
                    if j > 0:
                        low_split(YA[:, 1, j - 1], V2[:, (j - 1) % 2], YA[:, 0, j - 1], e + j - 1)
                u += 16
                e += 8
                for j in range(8):
                    dve.wait_ge(unit_done, u + j + 1)
                    dve.tensor_tensor(row2(XT[:, j, 0:T2]), row2(XT[:, j, 0:T2]), two(u + j), ALU.add).then_inc(psum_read, 1)
                u += 8
                dve.wait_ge(unit_done, u + 1)
                R16 = slice(0, HEADS)
                dve.tensor_scalar(row2(DTR[R16, 0]), two(u)[R16], col("dt_bias", 0, 1, HEADS), None, ALU.add).then_inc(psum_read, 1)
                dve.wait_ge(psum_read, pr + 9)
                dve.scalar_tensor_tensor(DTR[R16, 1], DTR[R16, 0], -1.0, DTR[R16, 0], ALU.mult, ALU.max).then_inc(dt_abs, 1)
                dve.wait_ge(dt_abs, 1)
                softplus(DTR[R16, 0], DTR[R16, 1], DTR[R16, 2], DTR[R16, 3], DTR[R16, 4], DTR[R16, 5], dt_exp, 2)
                step(dve.tensor_scalar(LAM[R16, 0, 1:2], LAM[R16, 0, 0:1], -1.0, None, ALU.mult))
                step(dve.tensor_scalar(DTR[R16, 1], DTR[R16, 0], LAM[R16, 0, 1:2], None, ALU.mult))
                for i, (a, z) in enumerate(SSD_TILES):
                    o, w = SSD_OFF[i], z - a
                    step(dve.tensor_tensor_scan(CUM[R16, o:o + w], col("ones", 0, w, HEADS), DTR[R16, 1, a:z], 0.0, ALU.mult, ALU.add))
                    if z < T2:
                        step(dve.tensor_tensor_scan(CUM[R16, o + w:o + T2 - a], col("ones", 0, 1, HEADS).broadcast_to([HEADS, T2 - z]),
                                                    DTR[R16, 1, z:T2], 0.0, ALU.mult, ALU.add))
                    step(dve.tensor_scalar(DTR[R16, 2, a:z], CUM[R16, o:o + w], -1.0, None, ALU.mult))
                    ins = dve.tensor_scalar(DTR[R16, 3, a:z], DTR[R16, 2, a:z], CUM[R16, o + w - 1:o + w], None, ALU.add)
                ins.then_inc(dt_rows, 1)
                dve.wait_ge(v_split, e)
                step(dve.memset(PAD[:, :, 0:3], 0.0))
                for j in range(12):
                    if j >= 2:
                        dve.wait_ge(xbc_ready, j - 1)
                    conv(CV[:, j % 2], j, 8 + j, lambda m, t: col("ssd_cw", t * 12 + m), lambda m: col("ssd_cb", m), j)
                dve.wait_ge(dt_cols, 1)
                p3 = PS[:, 2, 0:240].rearrange("p (a b c) -> p a b c", a=3, b=5)
                for a_ in range(3):
                    dve.tensor_copy(COLS[:, a_, 0:4], p3[:, a_, 0:4])
                step(dve.tensor_copy(COLS[0:16, :, 4], p3[0:16, :, 4]))
                for i, (a, z) in enumerate(SSD_TILES):
                    dve.wait_ge(xdt_mm, i + 1)
                    R = z - a
                    dve.tensor_tensor(XDT[0:R, i].rearrange("p (h d) -> p h d", d=HD),
                                      PS[0:R, i % 2].rearrange("p (h d) -> p h d", d=HD),
                                      COLS[0:R, 2, i].unsqueeze(2).broadcast_to([R, HEADS, HD]), ALU.mult).then_inc(xdt_ready, 1)

                def mask(s_):
                    i = s_ % 5
                    a, z = SSD_TILES[i]
                    dve.wait_ge(bc_mm, s_ + 1)
                    if s_ >= 2:
                        dve.wait_ge(w_ready, s_ - 1)
                    dve.tensor_tensor(EE[0:z - a, s_ % 2, 0:z - a], PS[0:z - a, s_ % 2, 0:z - a],
                                      col("ssd_mask", 0, z - a, z - a), ALU.add).then_inc(masked, 1)

                for s_ in range(-1, 80):
                    if s_ + 1 < 80 and s_ != 39:
                        mask(s_ + 1)
                    if s_ < 0:
                        continue
                    h, i = s_ // 5, s_ % 5
                    a, z = SSD_TILES[i]
                    R = z - a
                    dve.wait_ge(e_ready, s_ + 1)
                    dve.wait_ge(cb_read, 5 * (h // 8) + i + 1)
                    if s_ >= 2:
                        dve.wait_ge(ssd_y, s_ - 1)
                    dve.tensor_tensor(WW[0:R, s_ % 2, 0:T2 - a], EE[0:R, s_ % 2, 0:T2 - a], CB[0:R, SSD_OFF[i]:SSD_OFF[i] + T2 - a],
                                      ALU.mult).then_inc(w_ready, 1)
                    if h % 2 == 1 and i == 4:
                        m = h // 2
                        dve.wait_ge(ssd_y, s_ + 1)
                        dve.scalar_tensor_tensor(XS[:, m], XS[:, m], col("ssd_d", m), PS[:, 2 + m % 2, 0:T2], ALU.mult,
                                                 ALU.add).then_inc(y_read, 1)
                        dve.wait_ge(y_read, m + 1)
                        dve.tensor_tensor(XS[:, m], XS[:, m], Z[:, m], ALU.mult).then_inc(gated, 1)
                        dve.wait_ge(sq_ready, SQB + 8 + m + 1)
                        dve.wait_ge(sq_added, SQB + 8 + m)
                        if m % 4 == 0:
                            dve.tensor_copy(ACC2[:, m // 4], SQ2[:, m % 2]).then_inc(sq_added, 1)
                        else:
                            dve.tensor_tensor(ACC2[:, m // 4], ACC2[:, m // 4], SQ2[:, m % 2], ALU.add).then_inc(sq_added, 1)
                    if s_ == 39:
                        mask(40)
                u += 21
                rstd(Q2 + 1, u + 3, T2, 4 * P, DG2)
                dve.wait_ge(rb_ready, Q2 + 2)
                rstd(Q2 + 2, u + 3, T2, 4 * P, DG2)
                dve.wait_ge(rb_ready, Q2 + 3)
                dve.wait_ge(gated, 8)
                for k in range(DT + 1):
                    if k < DT:
                        v_free(e + k)
                        step(dve.tensor_tensor(TN2[:, k % 2], XS[:, k], PS[:, (u + 2 + k // 4) % 4, 0:T2], ALU.mult))
                        dve.tensor_scalar(V2[:, k % 2], TN2[:, k % 2], col("ssd_norm", k), None, ALU.mult).then_inc(v_ready, 1)
                    if k > 0:
                        low_split(H2[:, 1, k - 1], V2[:, (k - 1) % 2], H2[:, 0, k - 1], e + k - 1)
                residual(u, 16, T2, 8)

            def residual(u, sqn, T, xr):
                for j in range(8):
                    dve.wait_ge(unit_done, u + j + 1)
                    if T == T2:
                        dve.tensor_tensor(row2(XT[:, j, 0:T2]), row2(XT[:, j, 0:T2]), two(u + j), ALU.add).then_inc(resid_ready, 1)
                    else:
                        dve.tensor_tensor(XT[:, j, META:T2], XT[:, j, META:T2], PS[:, (u + j) % 4, 0:SEQ], ALU.add).then_inc(resid_ready, 1)
                    sq = SQB + sqn + j
                    dve.wait_ge(sq_ready, sq + 1)
                    dve.wait_ge(sq_added, sq)
                    if j == 0:
                        dve.tensor_copy(ACC[:, 0:T], SQ2[:, 0, 0:T]).then_inc(sq_added, 1)
                    else:
                        dve.tensor_tensor(ACC[:, 0:T], ACC[:, 0:T], SQ2[:, j % 2, 0:T], ALU.add).then_inc(sq_added, 1)

            def odd_layer():
                u, e = U2 + 53, E2 + 24
                dve.wait_ge(resid_ready, XR2 + 8)
                pre_plain(Q2 + 3, u, T2, "odd_norm", e)
                e += 8
                pr = PR2 + 9
                dve.wait_ge(unit_done, u + 1)
                dve.tensor_copy(row2(KK[:, 0]), two(u)).then_inc(psum_read, 1)
                for j in range(1, 9, 2):
                    dve.wait_ge(unit_done, u + j + 2)
                    t = token_psum(u + j, 5)
                    c = (j - 1) * P
                    dve.tensor_copy(VV[0:META, 0, c:c + 2 * P], t[0:META, 0])
                    dve.tensor_copy(VV[:, 1:5, c:c + 2 * P], t[:, 1:5]).then_inc(psum_read, 2)
                for j in range(9, 16):
                    dve.wait_ge(unit_done, u + j + 1)
                    dve.tensor_copy(row2(KK[:, j - 8]), two(u + j)).then_inc(psum_read, 1)
                for j in range(16, 24):
                    dve.wait_ge(unit_done, u + j + 1)
                    dve.tensor_copy(QQ[:, j - 16], PS[:, (u + j) % 4, 0:SEQ]).then_inc(psum_read, 1)
                dve.wait_ge(v_hi, e)
                step(dve.memset(WC[:, :, 0:1], 0.0))
                for i in range(-2, 65):
                    if 0 <= i - 1 < 64:
                        a = i - 1
                        nt = a % 4 + 1
                        dve.wait_ge(wt_mm, a + 1)
                        if a >= 2:
                            dve.wait_ge(sb_pv, a - 1)
                        dve.tensor_copy(WT[0:META, a % 2, 0:P], PS[0:META, 2, 0:P])
                        dve.tensor_copy(WT[:, a % 2, P:P + nt * P], PS[:, 2, P:P + nt * P]).then_inc(wt_read, 1)
                    if 0 <= i + 1 < 64:
                        a = i + 1
                        x = META + P * (a % 4 + 1)
                        wa, wb, wc = WA[:, a % 3], WB[:, a % 2], WC[:, a % 2]
                        dve.wait_ge(relu_ready, a + 1)
                        dve.wait_ge(ln_ready, a + 1)
                        dve.tensor_tensor(wa[:, x - P:x], wa[:, x - P:x], col("sb_keep", 0, P), ALU.mult)
                        step(dve.tensor_tensor(wb[:, x - P:x], wb[:, x - P:x], col("sb_keep", 0, P), ALU.mult))
                        step(dve.tensor_tensor_scan(wc[:, 1:x + 1], wa[:, 0:x], wb[:, 0:x], 0.0, ALU.add, ALU.add))
                        dve.tensor_scalar(SM[:, a % 3, 1:2], wc[:, x:x + 1], -1.0, None, ALU.mult)
                        step(dve.scalar_tensor_tensor(wa[:, 0:x], PS[:, a % 2, 0:x], QSCALE, wc[:, 0:x], ALU.mult, ALU.add))
                        dve.tensor_tensor(wa[:, x - P:x], wa[:, x - P:x], col("sb_mask", 0, P), ALU.add).then_inc(logw_ready, 1)
                    if i + 2 < 64:
                        a = i + 2
                        x = META + P * (a % 4 + 1)
                        dve.wait_ge(z_mm, a + 1)
                        if a >= 3:
                            dve.wait_ge(wt_mm, a - 2)
                        dve.wait_ge(abs_ready, a + 1)
                        dve.tensor_scalar(WA[:, a % 3, 0:x], PS[:, a % 2, 0:x], QSCALE, 0.0, ALU.mult, ALU.max).then_inc(relu_ready, 1)
                    if i >= 9 and (i - 1) % 8 == 0 or i == 64:
                        m = (i - 1) // 8 - 1 if i < 64 else 7
                        sb_out(m, e)
                u += 32
                dve.wait_ge(v_split, e + 8)
                residual(u, 24, SEQ, 16)
                rstd(Q2 + 4, u + 8, SEQ)
                dve.wait_ge(rb_ready, Q2 + 5)
                dve.wait_ge(resid_ready, XR2 + 16)
                for k in range(DT):
                    step(dve.tensor_tensor(FIN[:, k], XT[:, k, META:T2], PS[:, (u + 11) % 4, 0:SEQ], ALU.mult))
                    dve.tensor_scalar(FIN[:, k], FIN[:, k], col("final_norm", k), None, ALU.mult).then_inc(final_ready, 1)

            def sb_out(m, e):
                dve.wait_ge(sb_pv, 8 * m + 8)
                dve.wait_ge(silu_ready, SI2 + 24)
                v_free(e + m)
                dve.tensor_tensor(V3[:, m % 2], PS[:, 3, 0:SEQ], SG[:, m], ALU.mult).then_inc(v_ready, 1)
                low_split(H3[:, 1, m], V3[:, m % 2], H3[:, 0, m], e + m)

            for i, s in enumerate((psum_read, v_ready, v_split, sq_added, resid_ready, s_max, s_norm)):
                dve.memset(PRM[:, 5 + i:6 + i], 0.0).then_inc(s, PRIME)
            for s in (psum_read, v_ready, v_split, sq_added, resid_ready, s_max, s_norm):
                dve.wait_ge(s, PRIME)
            step(dve.memset(ST[:], 1.0))
            add_squares(T1, PRIME)
            with dve.Fori(0, MOD_CHUNKS // 3) as i:
                for s in range(3):
                    dve.wait_ge(mod_used, i * 3 + (s + 1))
                    dve.wait_ge(mod_tr, i * 3 + (s + 1))
                    dve.tensor_copy(MROW[0:2, s], PS[0:2, s, 0:SEQ]).then_inc(mod_row, 1)
            dve.wait_ge(mod_tr, MOD_CHUNKS + 3)
            dve.wait_ge(const_in, 16)
            step(dve.tensor_tensor(MODS[:], PS[:, 3, 0:288].rearrange("p (a c) -> p a c", c=2),
                                   col("b_mod", 0, 144).unsqueeze(2).broadcast_to([P, 144, 2]), ALU.add))
            for l in range(DEPTH):
                for s in range(3):
                    j = l * 72 + (3 * s + 1) * 8
                    g = (l * 3 + s) * 8
                    dve.scalar_tensor_tensor(MODS[:, j:j + 8], MODS[:, j:j + 8], 1.0,
                                             col("g_pre", g, 8).unsqueeze(2).broadcast_to([P, 8, 2]), ALU.add, ALU.mult)
                    j += 8
                    step(dve.scalar_tensor_tensor(MODS[:, j:j + 8], MODS[:, j:j + 8], 1.0 if s == 1 else 0.5,
                                                  col("g_post", g, 8).unsqueeze(2).broadcast_to([P, 8, 2]), ALU.mult, ALU.mult))
            for sub in subs:
                b = sub["in"]
                pre(sub, b, b["u"])
                if sub["kind"] == "ffn":
                    ffn(sub, b)
                    un = b["u"] + 68
                else:
                    mix(sub, b)
                    un = b["u"] + 24
                post(sub, b, un)
            if whole:
                even_layer()
                odd_layer()

        @block.tensor
        def _(pe):
            def stat(q, sq, un, T, ACC=ACC, DG=DG, rb=None):
                rb = (un + 3) % 4 if rb is None else rb % 4
                R, nt = (P, T // P) if T % P == 0 else (88, 6)
                pe.wait_ge(sq_added, sq)
                for j in range(nt):
                    ins = pe.matmul(PS[0:R, (un + 2) % 4, j:j + 1], ACC[:, j * R:j * R + R], col("ones"), start=True, stop=True)
                ins.then_inc(tot_ready, 1)
                pe.wait_ge(diag_ready, q + 1)
                for a in range(0, T, SEQ):
                    z = min(T, a + SEQ)
                    ins = pe.matmul(PS[:, rb, a:z], col("ones", 0, P, R), DG[0:R, a:z], start=True, stop=True)
                ins.then_inc(rb_ready, 1)

            def unit(u, i, j, src, T, KT, wait, ready=None, cap=DT, t0=0):
                s, pair = (u + j) % 2, (u + j) % 4
                pe.wait_ge(w_split, i * 4 + (u + j + 1))
                for semaphore, value in wait:
                    pe.wait_ge(semaphore, value)
                for k in range(KT):
                    if ready is not None:
                        pe.wait_ge(v_split, ready + min(k, cap - 1) + 1)
                    for n_, (wp, xp) in enumerate(((0, 0), (0, 1), (1, 0))):
                        for a, z in spans(T):
                            ins = pe.matmul(PS[:, pair, PSO[a]:PSO[a] + z - a], SPL[:, s, wp, k], src[:, xp, k, t0 + a:t0 + z],
                                            start=k == 0 and n_ == 0, stop=k == KT - 1 and n_ == 2)
                ins.then_inc(unit_done, 1)

            def token_units(u, src, tiles):
                pe.wait_ge(w_split, u + 2)
                for t, (tok, _) in enumerate(tiles):
                    o = (u % 4) * 1024 + t * 2 * P
                    for k in range(DT):
                        for n_, (xp, wp) in enumerate(((0, 0), (0, 1), (1, 0))):
                            ins = pe.matmul(PSF[:, o:o + 2 * P].rearrange("p (a c) -> p a c", a=2),
                                            src[:, xp, k, tok:tok + P], SPL[:, :, wp, k],
                                            start=k == 0 and n_ == 0, stop=k == DT - 1 and n_ == 2)
                ins.then_inc(unit_done, 2)

            def out_units(u, pr, src, T, KT, entry, ready, cap=DT):
                with pe.Fori(0, 2) as i:
                    for j in range(4):
                        unit(u, i, j, src, T, KT, [entry[j], (psum_read, i * 4 + (pr + j - 3))],
                             ready=ready if j == 0 else None, cap=cap)

            def ffn(sub, b):
                T = sub["T"]
                u, e, silu, pr = b["u"], b["e"] + 8, b["silu"], b["pr"]
                entry = [(psum_read, pr)] * 4
                for part, (f0, nf) in enumerate(F_PARTS):
                    with pe.Fori(0, nf // 2) as i:
                        for j in range(4):
                            free = (silu_ready, i * 2 + (silu + j - 1)) if j < 2 else (v_ready, i * 2 + (e + j - 3))
                            unit(u, i, j, H, T, DT, [entry[j], free], ready=b["e"] if part == 0 and j == 0 else None)
                    u += 2 * nf
                    e += nf
                    silu += nf
                    entry = [(silu_ready, silu - 1), (silu_ready, silu), (v_ready, e - 1), (v_ready, e)]
                    out_units(u, pr, G, T, nf, entry, e - nf)
                    u += 8
                    pr += 8
                    entry = [(psum_read, pr - 3 + j) for j in range(4)]

            def mix(sub, b):
                T, l = sub["T"], sub["l"]
                u, e, a0, mx, pr = b["u"], b["e"] + 8, b["att"], b["mix"], b["pr"]
                for j in range(10):
                    unit(u, 0, j, H, T if j in (0, 1, 2, 6, 7, 8) else T1, DT, [(psum_read, pr + j - 3)],
                         ready=b["e"] if j == 0 else None)
                for j in range(10, 16, 2):
                    pe.wait_ge(psum_read, pr + j - 2)
                    token_units(u + j, H, [(t * P, t * P) for t in range((T if j >= 14 else T1) // P)])
                pe.wait_ge(psum_read, pr + 16)
                for r in range(4):
                    pe.matmul(PS[:, r, 0:SEQ], col("rope_rot", 0, P), QK[:, 6 + r, 0:SEQ], start=True, stop=True)\
                      .then_inc(rope_rot, 1)
                pe.wait_ge(tab_in, 48 * (mx + 1))
                for r in range(4):
                    dt, trig = r // 2, r % 2
                    pe.wait_ge(rope_done, 4 * mx + r + 1)
                    for t in range(4):
                        ins = pe.matmul(PS[:, r, 0:SEQ], VT[:, t, SEQ + dt * P:SEQ + dt * P + P], FC[:, trig, t],
                                        start=t == 0, stop=t == 3)
                    if T == T1:
                        for t in range(2):
                            ins = pe.matmul(PS[:, r, SEQ:T1], VT[:, 4 + t, SEQ + dt * P:SEQ + dt * P + P],
                                            FCC[:, trig, t], start=t == 0, stop=t == 1)
                    ins.then_inc(four_a_s, 1)
                for dt in range(2):
                    pe.wait_ge(four_ev, 4 * mx + 2 * dt + 2)
                    for a in range(0, T, SEQ):
                        z = min(T, a + SEQ)
                        pe.matmul(PS[:, dt, a:z], col("four_cos", 0, P), FA[:, 2 * dt, a:z], start=True, stop=False)
                        ins = pe.matmul(PS[:, dt, a:z], col("four_sin", 0, P), FA[:, 2 * dt + 1, a:z], start=False, stop=True)
                    ins.then_inc(four_b_s, 1)
                pe.wait_ge(four_ev, 4 * (mx + 1))
                pe.wait_ge(v_ready, e + 2)
                e += 2
                steps = att_steps(sub)
                N = len(steps)

                def scores(i):
                    st, a = steps[i], a0 + i
                    pe.wait_ge(s_max, a - 1)
                    pe.wait_ge(s_ctx, a - 1)
                    q = QK[st["rows"], st["q"], st["t"] * P:st["t"] * P + P]
                    if st["lat"]:
                        k0, k1 = st["lat"]
                        pe.matmul(PS[:, a % 2, 0:k1 - k0], q, QK[st["rows"], st["k"], k0:k1], start=True, stop=True)
                    pe.matmul(PS[:, a % 2, SEQ:T1], q, QK[st["rows"], st["k"], SEQ:T1], start=True, stop=True).then_inc(s_mm, 1)

                def values(i):
                    st, a = steps[i], a0 + i
                    if i == 0 or steps[i - 1]["last"]:
                        pe.wait_ge(v_ready, e + st["ot"])
                    pe.wait_ge(s_trc, a + 1)
                    o = PS[st["rows"], 3, st["t"] * P:st["t"] * P + P]
                    nt = len(st["tt"])
                    for x, tt in enumerate(st["tt"]):
                        ins = pe.matmul(o, VT[:, tt, st["vcol"]:st["vcol"] + HD], PT[:, a % 2, x * P:x * P + P],
                                        start=x == 0, stop=x == nt - 1)
                    ins.then_inc(s_pv, 1)

                scores(0)
                scores(1)
                for i in range(N + 1):
                    if i + 2 < N:
                        scores(i + 2)
                    if i < N:
                        st, a = steps[i], a0 + i
                        pe.wait_ge(s_norm, a + 1)
                        pe.wait_ge(s_trc, a)
                        for x in range(len(st["tt"])):
                            ins = pe.transpose(PS[:, 2, x * P:x * P + P], SB[:, a % 3, 1 + x * P:1 + x * P + P], col("ident", 0, P))
                        ins.then_inc(s_tr, 1)
                    if i >= 1:
                        values(i - 1)
                pe.wait_ge(s_trc, a0 + N)
                pe.wait_ge(s_max, a0 + N)
                out_units(u + 16, pr + 16, H, T, DT, [(v_ready, e + 6)] * 4, e, cap=6)

            def loop_units(u, times, src, T, entry, free, ready=None, t0=0):
                with pe.Fori(0, times) as i:
                    for j in range(4):
                        unit(u, i, j, src, T, DT, [entry[j], (free[0], i * 4 + (free[1] + j - 3))],
                             ready=ready if j == 0 else None, t0=t0)

            def even_layer():
                u, e, pr = U2, E2, PR2
                stat(Q2, SQB + 8, u, T2)
                loop_units(u, 2, H2, T2, [(psum_read, pr - 3 + j) for j in range(4)], (pad_ready, PRIME), ready=e)
                u += 8
                e += 8
                pe.wait_ge(gate_w_in, 32)
                pe.wait_ge(pad_ready, PRIME + 8)
                for m in range(8):
                    g, t = m // 2, m % 2
                    pe.wait_ge(conv_done, 2 * g + 2)
                    if m >= 2:
                        pe.wait_ge(gate_read, 2 * (m - 1))
                    for x, gw in enumerate((GWA, GWX)):
                        for k in range(2):
                            for a, z in spans(T2):
                                ins = pe.matmul(PS[:, 2 * (m % 2) + x, PSO[a]:PSO[a] + z - a], gw[:, g, k, t],
                                                LX[:, 2 * g + k, a:z], start=k == 0, stop=k == 1)
                        ins.then_inc(gate_mm, 1)
                loop_units(u, 2, H2, T2, [(gate_read, 16)] * 4, (silu_ready, SI2))
                u += 8
                e += 8
                loop_units(u, 2, YA, T2, [(silu_ready, SI2 + 5 + j) for j in range(4)], (psum_read, pr), ready=e - 8)
                pr += 8
                u += 8
                unit(u, 0, 0, H2, T2, DT, [(psum_read, pr - 3)])
                u += 1
                pr += 1
                loop_units(u, 3, H2, T2, [(psum_read, pr)] * 4, (pad_ready, PRIME + 8))
                u += 12
                loop_units(u, 2, H2, T2, [(pad_ready, PRIME + 17 + j) for j in range(4)], (silu_ready, SI2 + 8))
                u += 8
                pe.wait_ge(silu_ready, SI2 + 16)
                pe.wait_ge(dt_rows, 1)
                for x, row in enumerate((2, 3, 0)):
                    for i, (a, z) in enumerate(SSD_TILES):
                        ins = pe.transpose(PS[0:z - a, 2, (x * 5 + i) * 16:(x * 5 + i) * 16 + 16], DTR[0:HEADS, row, a:z],
                                           col("ident", 0, HEADS, HEADS))
                ins.then_inc(dt_cols, 1)
                pe.wait_ge(xbc_ready, 8)
                for i, (a, z) in enumerate(SSD_TILES):
                    if i >= 2:
                        pe.wait_ge(xdt_ready, i - 1)
                    for m in range(DT):
                        ins = pe.transpose(PS[0:z - a, i % 2, m * P:m * P + P], XS[:, m, a:z], col("ident", 0, P))
                    ins.then_inc(xdt_mm, 1)
                pe.wait_ge(xdt_ready, 5)
                pe.wait_ge(xbc_ready, 12)

                def decay(s_):
                    h, i = s_ // 5, s_ % 5
                    a, z = SSD_TILES[i]
                    if s_ % 40 == 0:
                        pe.wait_ge(cb_read, 5 * (h // 8) + 5)
                    if s_ >= 2:
                        pe.wait_ge(e_ready, s_ - 1)
                    sel = col("ident", h, 1, HEADS).broadcast_to([HEADS, P])
                    for b0 in range(0, T2 - a, SEQ):
                        b1 = min(T2 - a, b0 + SEQ)
                        ins = pe.matmul(PS[:, s_ % 2, b0:b1], sel, CUM[0:HEADS, SSD_OFF[i] + b0:SSD_OFF[i] + b1], start=True, stop=True)
                    ins.then_inc(bc_mm, 1)

                for g in range(2):
                    for i, (a, z) in enumerate(SSD_TILES):
                        c = 5 * g + i
                        if i >= 2:
                            pe.wait_ge(cb_read, c - 1)
                        elif g == 1:
                            pe.wait_ge(e_ready, 40)
                        for b0 in range(a, T2, SEQ):
                            b1 = min(T2, b0 + SEQ)
                            ins = pe.matmul(PS[0:z - a, c % 2, b0 - a:b1 - a], BC[:, g, a:z], BC[:, 2 + g, b0:b1], start=True, stop=True)
                        ins.then_inc(cb_mm, 1)
                    decay(40 * g)
                    for s_ in range(40 * g, 40 * g + 40):
                        if s_ + 1 < 40 * g + 40:
                            decay(s_ + 1)
                        h, i = s_ // 5, s_ % 5
                        a, z = SSD_TILES[i]
                        m = h // 2
                        if h % 2 == 0 and i == 0 and m >= 2:
                            pe.wait_ge(y_read, m - 1)
                        pe.wait_ge(w_ready, s_ + 1)
                        rows = slice((h % 2) * HD, (h % 2) * HD + HD)
                        for b0, b1 in ((a, SEQ), (max(a, SEQ), T2)):
                            if b0 < b1:
                                ins = pe.matmul(PS[rows, 2 + m % 2, b0:b1], XDT[0:z - a, i, h * HD:h * HD + HD],
                                                WW[0:z - a, s_ % 2, b0 - a:b1 - a], start=i == 0, stop=i == 4 or (i == 3 and b1 == SEQ))
                        ins.then_inc(ssd_y, 1)
                pe.wait_ge(y_read, 8)
                stat(Q2 + 1, SQB + 12, u + 3, T2, ACC2[:, 0], DG2, u + 2)
                stat(Q2 + 2, SQB + 16, u + 3, T2, ACC2[:, 1], DG2, u + 3)
                loop_units(u, 2, H2, T2, [(v_ready, e + 8)] * 4, (resid_ready, XR2), ready=e)

            def odd_layer():
                u, e = U2 + 53, E2 + 24
                stat(Q2 + 3, SQB + 24, u, T2)
                pr = PR2 + 9
                unit(u, 0, 0, H2, T2, DT, [(resid_ready, XR2 + 8)], ready=e)
                e += 8
                for j in range(1, 9, 2):
                    pe.wait_ge(psum_read, pr + max(1, j - 2) if j > 1 else pr)
                    token_units(u + j, H2, [(0, 0)] + [(META + P * t, 0) for t in range(4)])
                unit(u, 0, 9, H2, T2, DT, [(psum_read, pr + 9)])
                unit(u, 0, 10, H2, T2, DT, [(psum_read, pr + 9)])
                unit(u, 0, 11, H2, T2, DT, [(psum_read, pr + 9)])
                loop_units(u + 12, 1, H2, T2, [(psum_read, pr + 9)] * 4, (psum_read, pr + 12))
                loop_units(u + 16, 2, H2, SEQ, [(psum_read, pr + 13 + j) for j in range(4)], (psum_read, pr + 16), t0=META)
                loop_units(u + 24, 2, H2, SEQ, [(psum_read, pr + 21 + j) for j in range(4)], (silu_ready, SI2 + 16), t0=META)
                pe.wait_ge(silu_ready, SI2 + 24)
                pe.wait_ge(psum_read, pr + 24)

                def scores(a):
                    h, i = a // 4, a % 4
                    rows = slice((h % 2) * HD, (h % 2) * HD + HD)
                    x = META + P * (i + 1)
                    if a >= 2:
                        pe.wait_ge(logw_ready, a - 1)
                    for b0 in range(0, x, SEQ):
                        b1 = min(x, b0 + SEQ)
                        ins = pe.matmul(PS[:, a % 2, b0:b1], QQ[rows, h // 2, i * P:i * P + P], KK[rows, h // 2, b0:b1], start=True, stop=True)
                    ins.then_inc(z_mm, 1)

                scores(0)
                scores(1)
                for a in range(65):
                    if a + 2 < 64:
                        scores(a + 2)
                    if a < 64:
                        i = a % 4
                        pe.wait_ge(weight_ready, a + 1)
                        if a >= 1:
                            pe.wait_ge(wt_read, a)
                        pe.transpose(PS[0:META, 2, 0:P], WA[:, a % 3, 0:META], col("ident", 0, P))
                        for t in range(i + 1):
                            ins = pe.transpose(PS[:, 2, P + t * P:2 * P + t * P], WA[:, a % 3, META + t * P:META + t * P + P], col("ident", 0, P))
                        ins.then_inc(wt_mm, 1)
                    if a >= 1:
                        c = a - 1
                        h, i = c // 4, c % 4
                        m = h // 2
                        rows = slice((h % 2) * HD, (h % 2) * HD + HD)
                        if c % 8 == 0 and c > 0:
                            pe.wait_ge(v_ready, e + m)
                        pe.wait_ge(wt_read, c + 1)
                        o = PS[rows, 3, i * P:i * P + P]
                        pe.matmul(o, VV[0:META, 0, h * HD:h * HD + HD], WT[0:META, c % 2, 0:P], start=True, stop=False)
                        for t in range(i + 1):
                            ins = pe.matmul(o, VV[:, t + 1, h * HD:h * HD + HD], WT[:, c % 2, P + t * P:2 * P + t * P], start=False, stop=t == i)
                        ins.then_inc(sb_pv, 1)
                pe.wait_ge(wt_read, 64)
                pe.wait_ge(logw_ready, 64)
                u += 32
                loop_units(u, 2, H3, SEQ, [(v_ready, e + 8)] * 4, (resid_ready, XR2 + 8), ready=e)
                stat(Q2 + 4, SQB + 32, u + 8, SEQ)

            pe.wait_ge(const_in, 16)
            for s in (s_mm, s_tr, s_pv):
                pe.matmul(PS[0:1, 3, 0:1], col("ones"), col("ones"), start=True, stop=True).then_inc(s, PRIME)
            pe.wait_ge(cact_ready, 1)
            pe.matmul(PS[0:1, 3, 0:1], col("ones"), col("ones"), start=True, stop=True).then_inc(mod_tr, 3)

            def mod_rows(i, s):
                pe.wait_ge(mod_in[s], i * 16 + 16)
                for k in range(DT):
                    ins = pe.matmul(PS[0:2, s, 0:SEQ], col("cond", 2 * k, 2), MODRING[:, s, k], start=k == 0, stop=k == DT - 1)
                ins.then_inc(mod_used, 1)

            def mod_cols(i, s):
                pe.wait_ge(mod_row, i * 3 + (s + 1))
                for t in range(4):
                    ins = pe.matmul(PS[:, 3, bass.ds(i * 24 + (s * 8 + 2 * t), 2)], MROW[0:2, s, t * P:t * P + P],
                                    col("ident", 0, 2, 2), start=True, stop=True)
                ins.then_inc(mod_tr, 1)

            with pe.Fori(0, MOD_CHUNKS // 3) as i:
                mod_rows(i, 0)
                mod_rows(i, 1)
                mod_cols(i, 0)
                mod_rows(i, 2)
                mod_cols(i, 1)
                mod_cols(i, 2)
            for idx, sub in enumerate(subs):
                b = sub["in"]
                T = sub["T"]
                Tp = T1 if sub["kind"] == "mix" else T
                stat(b["q"], b["sq"] + 8, b["u"], Tp)
                if sub["kind"] == "ffn":
                    ffn(sub, b)
                    un = b["u"] + 68
                else:
                    mix(sub, b)
                    un = b["u"] + 24
                stat(b["q"] + 1, b["sq"] + 16, un, T)
            if whole:
                even_layer()
                odd_layer()

        @block.sync
        def _(sp):
            for m in range(DT):
                if whole:
                    sp.wait_ge(final_ready, m + 1)
                    sp.dma_start(out[:, m], FIN[:, m]).then_inc(out_sem, 16)
                else:
                    sp.wait_ge(resid_ready, end["xr"])
                    sp.dma_start(out[:, m], XT[:, m, META:META + SEQ]).then_inc(out_sem, 16)
            sp.wait_ge(out_sem, 16 * DT)


def feat(a):
    a = np.asarray(a).reshape(-1, P)
    return a.T


def constants(i):
    K = np.zeros((P, N_COL), np.float32)

    def put(name, a):
        o, w = COL[name]
        K[:a.shape[0], o:o + w] = a

    p = np.arange(P)
    put("ident", np.eye(P))
    put("ones", np.ones((P, P)))
    c = p % GRID_W
    kc = np.arange(GRID_W)[None, :]
    ws = np.clip(c - 8, 0, GRID_W - 16)[:, None]
    put("na_mask", np.where((kc >= ws) & (kc < ws + 16), 0.0, NEG))
    rel = np.arange(384)[None, :] - P - p[:, None]
    put("swa_mask", np.where(np.abs(rel) <= 128, 0.0, NEG))
    rot = np.zeros((P, P))
    for m in range(P):
        if m % 32 < 16:
            rot[m + 16, m] = -1.0
        else:
            rot[m - 16, m] = 1.0
    put("rope_rot", rot)
    d = p % HD
    same = (p[:, None] // HD) == (p[None, :] // HD)
    ang = 2 * np.pi * ((d[:, None] * d[None, :]) % HD) / HD
    put("four_cos", np.where(same, np.cos(ang), 0.0))
    put("four_sin", np.where(same, -np.sin(ang), 0.0))
    put("ssd_mask", np.where(p[None, :] < p[:, None], NEG, 0.0))
    put("sb_mask", np.where(p[None, :] >= p[:, None], NEG, 0.0))
    put("sb_keep", np.where(p[None, :] < p[:, None], 1.0, 0.0))
    put("g_pre", feat(i["g_pre"]))
    put("g_post", feat(i["g_post"]))
    put("b_mod", feat(i["b_mod"]))
    put("sink", np.broadcast_to(i["swa_sink"].reshape(1, 12), (P, 12)))
    for name, key in (("even_norm", "even_norm_2"), ("lru_cw", "lru_conv_w_2"), ("lru_cb", "lru_conv_b_2"),
                      ("lru_ba", "lru_b_a_2"), ("lru_bx", "lru_b_x_2"), ("lru_lam", "lru_lambda_2"),
                      ("ssd_cw", "ssd_conv_w_2"), ("ssd_cb", "ssd_conv_b_2"), ("ssd_norm", "ssd_norm_2"),
                      ("odd_norm", "odd_norm_2"), ("final_norm", "final_norm_2")):
        put(name, feat(i[key]))
    put("ssd_d", feat(np.repeat(i["ssd_d_2"].reshape(-1), HD)))
    put("dt_bias", i["ssd_dt_bias_2"].reshape(HEADS, 1))
    put("a_log", i["ssd_a_log_2"].reshape(HEADS, 1))
    put("cond", np.stack([i["c"].reshape(DT, P), i["c_ctx"].reshape(DT, P)], 1).reshape(16, P).T)
    return K


def dft(n):
    a = 2 * np.pi * ((np.arange(n)[:, None] * np.arange(n)[None, :]) % n) / n
    t = np.stack([np.cos(a), np.sin(a)]) / np.sqrt(n * HD)
    return np.ascontiguousarray(t.reshape(2, n // P, P, n).transpose(2, 0, 1, 3)).astype(np.float32)


def rope_tables():
    p = np.arange(P) % HD
    t = np.arange(SEQ)
    inv = np.float32(10000.0) ** (-(np.arange(16, dtype=np.float32)) / np.float32(16))
    pos = np.where(p[:, None] < 32, t[None, :] // GRID_W, t[None, :] % GRID_W).astype(np.float32)
    ang = pos * inv[p % 16][:, None].astype(np.float32)
    return np.stack([np.cos(ang), np.sin(ang)], 1).astype(np.float32)


def units_of(w):
    k, m = w.shape[0] // P, w.shape[1] // P
    u = np.zeros((m, P, DT, P), np.float32)
    u[:, :, :k] = w.reshape(k, P, m, P).transpose(2, 1, 0, 3)
    return u


def unit_stream(i):
    us = []

    def ffn(l, s):
        w1, w2 = i["w_ffn_in"][l, s], i["w_ffn_out"][l, s]
        gate, up = units_of(w1[:, :F_TILES * P]), units_of(w1[:, F_TILES * P:])
        for f0, nf in F_PARTS:
            for f in range(f0, f0 + nf, 2):
                us.extend([gate[f:f + 2], up[f:f + 2]])
            us.append(units_of(w2[f0 * P:(f0 + nf) * P]))

    for l in range(DEPTH):
        ffn(l, 0)
        w = i["w_in"][l]
        pair = np.concatenate([np.arange(h * HD, h * HD + HD) for h in (0, 3, 1, 4, 2, 5)])
        us.append(units_of(w[:, 0:768]))
        us.append(units_of(w[:, 1152:1536][:, pair]))
        us.append(units_of(w[:, 1536:1664]))
        us.append(units_of(w[:, 768:1152]))
        us.append(units_of(w[:, 1664:1792]))
        us.append(units_of(w[:, 1792:2048]))
        wo = i["w_out"][l]
        us.append(units_of(np.concatenate([wo[0:384], wo[384:768][pair], wo[768:]])))
        ffn(l, 1)
    w = i["even_w_in_2"][0]
    us.append(units_of(w[:, 0:2 * D]))
    us.append(units_of(i["even_w_out_2"][0][0:D]))
    dt = np.zeros((D, P), np.float32)
    dt[:, 0:HEADS] = w[:, 4608:4624]
    us.append(units_of(dt))
    us.append(units_of(w[:, 3072:4608]))
    us.append(units_of(w[:, 2048:3072]))
    us.append(units_of(i["even_w_out_2"][0][D:2 * D]))
    w = i["odd_w_in_2"][0]
    q, k, v, g = (units_of(w[:, n * D:n * D + D]) for n in range(4))
    us.extend([k[0:1], v, k[1:8], q, g])
    us.append(units_of(i["odd_w_out_2"][0]))
    us.append(us[0][0:2])
    return np.concatenate(us).reshape(-1, P, D)


def tiles_of(a):
    return np.ascontiguousarray(a.T.reshape(DT, P, -1).transpose(1, 0, 2))


STOP = 99


def kernel(**inputs):
    import concourse.bacc as bacc
    from concourse.bass_utils import run_bass_kernel_spmd

    i = inputs
    rpb = np.zeros((DEPTH * 6, 15, RPB_W), np.float32)
    rpb[..., 48:79] = i["na_rpb"].reshape(DEPTH * 6, 15, 31)
    off = np.arange(GRID_W)[None, :] - np.arange(GRID_W)[:, None] + GRID_W - 1
    rpb = np.ascontiguousarray(rpb[:, :, off].transpose(0, 2, 1, 3))
    arrays = {
        "xT": tiles_of(i["x"][0]), "ctxT": tiles_of(i["ctx"][0]), "metaT": tiles_of(i["meta_2"]),
        "const": constants(i),
        "modw": np.ascontiguousarray(i["w_mod"].reshape(DEPTH, DT, P, -1, SEQ).transpose(0, 3, 2, 1, 4)).reshape(
            MOD_CHUNKS, P, DT * SEQ),
        "wu": unit_stream(i), "rpb": rpb, "rope": rope_tables(), "four": dft(SEQ), "four_c": dft(CTX),
        "gatew": np.ascontiguousarray(np.stack([i["lru_w_a_2"][0], i["lru_w_x_2"][0]]).reshape(
            2, 4, 2, P, 2, P).transpose(3, 0, 1, 2, 4, 5)),
    }
    nc = bacc.Bacc("TRN2", target_bir_lowering=False, num_devices=1)
    args = {k: nc.dram_tensor(k + "_dram", v.shape, F32, kind="ExternalInput").ap() for k, v in arrays.items()}
    out = nc.dram_tensor("out_dram", (P, DT, SEQ), F32, kind="ExternalOutput").ap()
    build(nc, **args, out=out, stop=STOP)
    r = run_bass_kernel_spmd(nc, [{k + "_dram": v for k, v in arrays.items()}], core_ids=[0])
    o = r.results[0]["out_dram"]
    return np.ascontiguousarray(o.transpose(2, 1, 0)).reshape(1, SEQ, D)
```
